# Optimizing a Trainium2 kernel written in Bass

```python
import math
import jax
import jax.numpy as jnp
from jax import lax
import numpy as np

D_MODEL = 1024
BATCH = 1
SEQ = 256
DEPTH = 2
DEC_BATCH = 8
DEC_SEQ = 8
PAST_LEN = 1024
PAGE_SIZE = 128

N_A_LAYERS = DEPTH // 2
N_B_LAYERS = DEPTH - N_A_LAYERS
CONV_WIDTH = 31
CONV_STATE = CONV_WIDTH - 1
N_HEADS = 8
QK_NOPE = 128
QK_ROPE = 64
V_HEAD = 128
KV_LORA = 256
Q_LORA = 512
ROPE_BASE = 10000.0
Q_BLOCK = 128
SCORE_SCALE = (QK_NOPE + QK_ROPE) ** -0.5
N_EXPERTS = 16
N_GROUPS = 4
EXPERTS_PER_GROUP = N_EXPERTS // N_GROUPS
TOP_K = 2
D_EXPERT = 512
ALPHA = (2 * DEPTH) ** 0.25
BETA = (8 * DEPTH) ** -0.25
LN_EPS = 1e-5
RMS_EPS = 1e-6

kernel_name = 'yoco_conformer_mla_groupmoe_step'

def layer_norm(x, g, b):
    xf = x.astype(jnp.float32)
    mu = jnp.mean(xf, axis=-1, keepdims=True)
    var = jnp.mean(jnp.square(xf - mu), axis=-1, keepdims=True)
    y = (xf - mu) * lax.rsqrt(var + LN_EPS)
    return (y * g.astype(jnp.float32) + b.astype(jnp.float32)).astype(x.dtype)

def rms_norm(x, g):
    xf = x.astype(jnp.float32)
    y = xf * lax.rsqrt(jnp.mean(jnp.square(xf), axis=-1, keepdims=True) + RMS_EPS)
    return (y * g.astype(jnp.float32)).astype(x.dtype)

def rope(x, pos):
    half = QK_ROPE // 2
    inv_freq = ROPE_BASE ** (-jnp.arange(half, dtype=jnp.float32) / half)
    ang = pos.astype(jnp.float32)[:, None] * inv_freq[None, :]
    cos = jnp.cos(ang)[:, None, :]
    sin = jnp.sin(ang)[:, None, :]
    xf = x.astype(jnp.float32)
    x1, x2 = xf[..., :half], xf[..., half:]
    return jnp.concatenate([x1 * cos - x2 * sin, x2 * cos + x1 * sin], axis=-1).astype(x.dtype)

def conv_module(x, past, w_pw1, b_pw1, w_dw, b_dw, g_cn, b_cn, w_pw2, b_pw2):
    h = x @ w_pw1 + b_pw1
    u = h[..., :D_MODEL] * jax.nn.sigmoid(h[..., D_MODEL:])
    ext = jnp.concatenate([past.astype(u.dtype), u], axis=1)
    conv = lax.conv_general_dilated(
        ext, w_dw[:, None, :].astype(ext.dtype), window_strides=(1,), padding='VALID',
        dimension_numbers=('NWC', 'WIO', 'NWC'), feature_group_count=D_MODEL) + b_dw
    z = layer_norm(conv, g_cn, b_cn)
    z = z * jax.nn.sigmoid(z)
    return z @ w_pw2 + b_pw2, ext[:, -CONV_STATE:]

def moe(x, r_w, r_b, w1, w3, w2):
    t = x.reshape(-1, D_MODEL)
    aff = jax.nn.sigmoid((t @ r_w).astype(jnp.float32))
    sel = aff + r_b.astype(jnp.float32)
    group_score = lax.top_k(sel.reshape(-1, N_GROUPS, EXPERTS_PER_GROUP), TOP_K)[0].sum(-1)
    g_star = jnp.argmax(group_score, axis=-1)
    in_group = (jnp.arange(N_EXPERTS) // EXPERTS_PER_GROUP)[None, :] == g_star[:, None]
    _, idx = lax.top_k(jnp.where(in_group, sel, -jnp.inf), TOP_K)
    w_sel = jnp.take_along_axis(aff, idx, axis=-1)
    w_sel = w_sel / jnp.sum(w_sel, axis=-1, keepdims=True)
    gates = jnp.einsum('tk,tke->te', w_sel, jax.nn.one_hot(idx, N_EXPERTS, dtype=jnp.float32))
    out = jnp.zeros(t.shape, jnp.float32)
    for e in range(N_EXPERTS):
        h = jax.nn.silu(t @ w1[e]) * (t @ w3[e])
        out = out + gates[:, e:e + 1] * (h @ w2[e]).astype(jnp.float32)
    return out.astype(x.dtype).reshape(x.shape)

def mla_shared_kv(h, pos, w_dkv, g_kv, w_kr):
    c_kv = rms_norm(h @ w_dkv, g_kv)
    k_pe = rope((h @ w_kr)[:, :, None, :], pos)[:, :, 0, :]
    return c_kv, k_pe

def mla_queries(x, pos, w_dq, g_q, w_uq, w_uk):
    c_q = rms_norm(x @ w_dq, g_q)
    q = jnp.einsum('bsr,rhd->bshd', c_q, w_uq)
    q_lat = jnp.einsum('bshd,rhd->bshr', q[..., :QK_NOPE], w_uk)
    q_pe = rope(q[..., QK_NOPE:], pos)
    return q_lat, q_pe

def attend_prompt(q_lat, q_pe, c_kv, k_pe):
    b, s = q_lat.shape[0], q_lat.shape[1]
    nb = s // Q_BLOCK
    ql = q_lat.reshape(b, nb, Q_BLOCK, N_HEADS, KV_LORA).transpose(1, 0, 2, 3, 4)
    qp = q_pe.reshape(b, nb, Q_BLOCK, N_HEADS, QK_ROPE).transpose(1, 0, 2, 3, 4)
    kpos = jnp.arange(s)

    def block(args):
        qlb, qpb, i = args
        sc = (jnp.einsum('bqhr,bkr->bhqk', qlb, c_kv)
              + jnp.einsum('bqhp,bkp->bhqk', qpb, k_pe)).astype(jnp.float32) * SCORE_SCALE
        qpos = i * Q_BLOCK + jnp.arange(Q_BLOCK)
        sc = jnp.where(kpos[None, :] <= qpos[:, None], sc, -jnp.inf)
        p = jax.nn.softmax(sc, axis=-1).astype(c_kv.dtype)
        return jnp.einsum('bhqk,bkr->bqhr', p, c_kv)

    o = lax.map(block, (ql, qp, jnp.arange(nb)))
    return o.transpose(1, 0, 2, 3, 4).reshape(b, s, N_HEADS, KV_LORA)

def attend_sample(q_lat, q_pe, c_past, kpe_past, c_new, kpe_new):
    t = q_lat.shape[1]
    n_past = c_past.shape[1]
    s_past = jnp.einsum('bqhr,bkr->bhqk', q_lat, c_past) + jnp.einsum('bqhp,bkp->bhqk', q_pe, kpe_past)
    s_new = jnp.einsum('bqhr,bkr->bhqk', q_lat, c_new) + jnp.einsum('bqhp,bkp->bhqk', q_pe, kpe_new)
    s_new = jnp.where(jnp.tril(jnp.ones((t, t), bool)), s_new.astype(jnp.float32), -jnp.inf)
    sc = jnp.concatenate([s_past.astype(jnp.float32), s_new], axis=-1) * SCORE_SCALE
    p = jax.nn.softmax(sc, axis=-1).astype(c_past.dtype)
    return (jnp.einsum('bhqk,bkr->bqhr', p[..., :n_past], c_past)
            + jnp.einsum('bhqk,bkr->bqhr', p[..., n_past:], c_new.astype(c_past.dtype)))

def trunk(x, pos, conv_past, kv_past, params):
    (a_w_pw1, a_b_pw1, a_w_dw, a_b_dw, a_g_cn, a_b_cn, a_w_pw2, a_b_pw2,
     ln_mix_g, ln_mix_b, ln_ffn_g, ln_ffn_b,
     b_w_dq, b_g_q, b_w_uq, b_w_o,
     s_w_dkv, s_g_kv, s_w_kr, s_w_uk, s_w_uv,
     r_w, r_b, e_w1, e_w3, e_w2) = params
    conv_new = []
    c_kv = None
    k_pe = None
    for l in range(DEPTH):
        if l < N_A_LAYERS:
            mix, buf = conv_module(x, conv_past[l], a_w_pw1[l], a_b_pw1[l], a_w_dw[l], a_b_dw[l],
                                   a_g_cn[l], a_b_cn[l], a_w_pw2[l], a_b_pw2[l])
            conv_new.append(buf)
        else:
            j = l - N_A_LAYERS
            if c_kv is None:
                c_kv, k_pe = mla_shared_kv(x, pos, s_w_dkv, s_g_kv, s_w_kr)
            q_lat, q_pe = mla_queries(x, pos, b_w_dq[j], b_g_q[j], b_w_uq[j], s_w_uk)
            if kv_past is None:
                o_lat = attend_prompt(q_lat, q_pe, c_kv, k_pe)
            else:
                o_lat = attend_sample(q_lat, q_pe, kv_past[0], kv_past[1], c_kv, k_pe)
            o = jnp.einsum('bshr,rhv->bshv', o_lat, s_w_uv)
            mix = o.reshape(o.shape[0], o.shape[1], N_HEADS * V_HEAD) @ b_w_o[j]
        x = layer_norm(ALPHA * x + mix, ln_mix_g[l], ln_mix_b[l])
        x = layer_norm(ALPHA * x + moe(x, r_w, r_b, e_w1[l], e_w3[l], e_w2[l]), ln_ffn_g[l], ln_ffn_b[l])
    return x, jnp.stack(conv_new), c_kv, k_pe

def setup_inputs(seed: int = 0) -> dict:
    key = jax.random.key(seed)
    ks = jax.random.split(key, 40)
    counter = iter(range(40))

    def nrm(shape, scale):
        return jax.random.normal(ks[next(counter)], shape, jnp.float32) * scale

    n_pages = PAST_LEN // PAGE_SIZE
    n_used = DEC_BATCH * n_pages
    n_pool = (n_used * 5) // 4
    d, f, e = D_MODEL, D_EXPERT, N_EXPERTS
    return {
        'x_prompt': nrm((BATCH, SEQ, d), 1.0),
        'x_sample': nrm((DEC_BATCH, DEC_SEQ, d), 1.0),
        'state_conv': nrm((N_A_LAYERS, DEC_BATCH, CONV_STATE, d), 0.5),
        'cache_ckv': nrm((n_pool, PAGE_SIZE, KV_LORA), 1.0),
        'cache_kpe': nrm((n_pool, PAGE_SIZE, QK_ROPE), 1.0),
        'page_table': jax.random.permutation(ks[next(counter)], n_pool)[:n_used].reshape(DEC_BATCH, n_pages).astype(jnp.int32),
        'a_w_pw1': nrm((N_A_LAYERS, d, 2 * d), d ** -0.5),
        'a_b_pw1': nrm((N_A_LAYERS, 2 * d), 0.02),
        'a_w_dw': nrm((N_A_LAYERS, CONV_WIDTH, d), CONV_WIDTH ** -0.5),
        'a_b_dw': nrm((N_A_LAYERS, d), 0.02),
        'a_g_cn': 1.0 + nrm((N_A_LAYERS, d), 0.02),
        'a_b_cn': nrm((N_A_LAYERS, d), 0.02),
        'a_w_pw2': nrm((N_A_LAYERS, d, d), BETA * d ** -0.5),
        'a_b_pw2': nrm((N_A_LAYERS, d), 0.02),
        'ln_mix_g': 1.0 + nrm((DEPTH, d), 0.02),
        'ln_mix_b': nrm((DEPTH, d), 0.02),
        'ln_ffn_g': 1.0 + nrm((DEPTH, d), 0.02),
        'ln_ffn_b': nrm((DEPTH, d), 0.02),
        'b_w_dq': nrm((N_B_LAYERS, d, Q_LORA), d ** -0.5),
        'b_g_q': 1.0 + nrm((N_B_LAYERS, Q_LORA), 0.02),
        'b_w_uq': nrm((N_B_LAYERS, Q_LORA, N_HEADS, QK_NOPE + QK_ROPE), Q_LORA ** -0.5),
        'b_w_o': nrm((N_B_LAYERS, N_HEADS * V_HEAD, d), BETA * (N_HEADS * V_HEAD) ** -0.5),
        's_w_dkv': nrm((d, KV_LORA), d ** -0.5),
        's_g_kv': 1.0 + nrm((KV_LORA,), 0.02),
        's_w_kr': nrm((d, QK_ROPE), d ** -0.5),
        's_w_uk': nrm((KV_LORA, N_HEADS, QK_NOPE), KV_LORA ** -0.5),
        's_w_uv': nrm((KV_LORA, N_HEADS, V_HEAD), BETA * KV_LORA ** -0.5),
        'r_w': nrm((d, e), d ** -0.5),
        'r_b': nrm((e,), 0.01),
        'e_w1': nrm((DEPTH, e, d, f), d ** -0.5),
        'e_w3': nrm((DEPTH, e, d, f), d ** -0.5),
        'e_w2': nrm((DEPTH, e, f, d), BETA * f ** -0.5),
    }

def reference(x_prompt, x_sample, state_conv, cache_ckv, cache_kpe, page_table,
              a_w_pw1, a_b_pw1, a_w_dw, a_b_dw, a_g_cn, a_b_cn, a_w_pw2, a_b_pw2,
              ln_mix_g, ln_mix_b, ln_ffn_g, ln_ffn_b,
              b_w_dq, b_g_q, b_w_uq, b_w_o,
              s_w_dkv, s_g_kv, s_w_kr, s_w_uk, s_w_uv,
              r_w, r_b, e_w1, e_w3, e_w2):
    params = (a_w_pw1, a_b_pw1, a_w_dw, a_b_dw, a_g_cn, a_b_cn, a_w_pw2, a_b_pw2,
              ln_mix_g, ln_mix_b, ln_ffn_g, ln_ffn_b,
              b_w_dq, b_g_q, b_w_uq, b_w_o,
              s_w_dkv, s_g_kv, s_w_kr, s_w_uk, s_w_uv,
              r_w, r_b, e_w1, e_w3, e_w2)
    b_p, s_p = x_prompt.shape[0], x_prompt.shape[1]
    conv0 = jnp.zeros((N_A_LAYERS, b_p, CONV_STATE, D_MODEL), x_prompt.dtype)
    y_prompt, conv_prompt, ckv_prompt, kpe_prompt = trunk(
        x_prompt, jnp.arange(s_p), conv0, None, params)
    b_s, t_s = x_sample.shape[0], x_sample.shape[1]
    c_past = cache_ckv[page_table].reshape(b_s, -1, KV_LORA)
    kpe_past = cache_kpe[page_table].reshape(b_s, -1, QK_ROPE)
    pos_s = c_past.shape[1] + jnp.arange(t_s)
    y_sample, conv_sample, ckv_sample, kpe_sample = trunk(
        x_sample, pos_s, state_conv, (c_past, kpe_past), params)
    return (y_prompt, y_sample, conv_prompt, conv_sample, ckv_prompt, kpe_prompt, ckv_sample, kpe_sample)


_drawn_inputs = setup_inputs


def setup_inputs(seed=0):
    import zlib

    import numpy as np

    out = dict(_drawn_inputs(seed))
    spreads = {}
    factors = {'cache_ckv': 4.538,
     'cache_kpe': 2.935,
     'a_g_cn': 2.797,
     'a_b_cn': 8.0,
     'b_g_q': 8.0,
     's_g_kv': 2.723}
    for name, (base, spread) in spreads.items():
        noise = np.random.default_rng([zlib.crc32(name.encode()), seed]).standard_normal(out[name].shape)
        drawn = base * np.exp(spread * noise) if base else spread * noise
        out[name] = jnp.asarray(drawn.astype(out[name].dtype))
    for name, factor in factors.items():
        out[name] = (out[name] * factor).astype(out[name].dtype)
    return out
```

```python
from contextlib import ExitStack

import numpy as np
import concourse.bass as bass
from concourse import mybir

F32 = mybir.dt.float32
I32 = mybir.dt.int32
ALU = mybir.AluOpType
ACT = mybir.ActivationFunctionType
AX = mybir.AxisListType

P = 128
D = 1024
KD = D // P
SEQ, DB, DS = 256, 8, 8
NS = DB * DS
T = SEQ + NS
TILES = [(0, 128), (128, 128), (256, 64)]
CW = 31
CS = CW - 1
EXTP = CS + SEQ
EXTS = CS + DS
NH, NOPE, ROPE, VH = 8, 128, 64, 128
KV, QR = 256, 512
HALF = ROPE // 2
PAST, PAGE = 1024, 128
NPG = PAST // PAGE
NPOOL = 80
SCALE = float((NOPE + ROPE) ** -0.5)
E, NG, EG, FE = 16, 4, 4, 512
DEPTH = 2
ALPHA = float((2 * DEPTH) ** 0.25)
LN_EPS, RMS_EPS = 1e-5, 1e-6
C = 64
CHUNKS = T // C
SLOTS = E * CHUNKS
BIG = 1e30


def tables():
    i = np.arange(P)
    ident = np.eye(P, dtype=np.float32)
    before = (i[:, None] < i[None, :]).astype(np.float32)
    pos = np.concatenate([np.arange(SEQ), np.tile(PAST + np.arange(DS), DB)]).astype(np.float32)
    inv = (np.float32(10000.0) ** (-np.arange(HALF, dtype=np.float32) / np.float32(HALF))).astype(np.float32)
    ang = (pos[:, None] * inv[None, :]).astype(np.float32).astype(np.float64)
    cos, sin = np.cos(ang).astype(np.float32), np.sin(ang).astype(np.float32)
    rope_T = np.zeros((P, 2, T), np.float32)
    rope_T[:, 0] = np.tile(cos.T, (4, 1))
    rope_T[:, 1] = np.tile(sin.T, (4, 1))
    rope_tok = np.zeros((P, 3, 2, HALF), np.float32)
    for n, (t0, m) in enumerate(TILES):
        rope_tok[:m, n, 0] = cos[t0:t0 + m]
        rope_tok[:m, n, 1] = sin[t0:t0 + m]
    swap = np.zeros((P, P), np.float32)
    for b in (0, ROPE):
        for j in range(HALF):
            swap[b + j + HALF, b + j] = -1.0
            swap[b + j, b + j + HALF] = 1.0
    causal = np.zeros((P, 3, P), np.float32)
    causal[:, 0] = causal[:, 2] = np.where(i[None, :] <= i[:, None], 0.0, -BIG)
    causal = causal.reshape(P, 3 * P)
    own = np.full((P, DB // 2, NS), -BIG, np.float32)
    for r in range(P):
        half, t = r // NS, r % DS
        for p in range(DB // 2):
            b = 2 * p + half
            own[r, p, b * DS:b * DS + t + 1] = 0.0
    f = np.arange(3 * E) % E
    route = np.zeros((P, 3, 3 * E), np.float32)
    route[:, 0] = E - f
    route[:, 1] = f * CHUNKS
    route[:, 2] = f // EG
    return dict(c_ident=ident, c_before=before, c_rope_T=rope_T, c_rope_tok=rope_tok, c_swap=swap,
                c_causal=causal, c_own=own, c_route=route)


def trunk_step(nc, a):
    VECS = [("a_b_pw1", 16), ("a_b_dw", 8), ("a_g_cn", 8), ("a_b_cn", 8), ("b_g_q", 4)]
    NVEC = sum(n for _, n in VECS)
    MISC = 9 * 16
    TAPS = 2 * (CW + 1)
    S_TAPS = 2 * (CW + 4)
    UB = [7, 4, 5, 7]
    MASK = 13
    MORE = 2 * T // C
    ZEROED = 2 * MORE * C // P
    OUT_STORES = 10
    ctx = ExitStack()
    with ctx:
        def sb(name, shape, dt=F32):
            return ctx.enter_context(nc.sbuf_tensor(name, shape, dt))

        def sem(name):
            return ctx.enter_context(nc.semaphore(name))

        def part(buf, at, *dims):
            n = int(np.prod(dims))
            v = buf[:, at:at + n]
            if len(dims) == 2:
                v = v.rearrange("p (a b) -> p a b", a=dims[0])
            elif len(dims) == 3:
                v = v.rearrange("p (a b c) -> p a b c", a=dims[0], b=dims[1])
            elif len(dims) == 4:
                v = v.rearrange("p (a b c d) -> p a b c d", a=dims[0], b=dims[1], c=dims[2])
            return v

        x_rows = [nc.dram_tensor(f"x_rows{l}", [T, D], F32).ap() for l in range(DEPTH)]
        slot_token = [nc.dram_tensor(f"slot_token{l}", [C * SLOTS, 1], I32).ap() for l in range(DEPTH)]
        y_rows = nc.dram_tensor("y_rows", [(E + MORE) * C, D], F32).ap()

        credit = nc.dram_tensor("credit", [4, P], F32).ap()

        w13 = [sb(f"w13_{s}", [P, 2 * KD * FE]) for s in range(2)]
        w2 = [sb(f"w2_{s}", [P, 4 * D]) for s in range(2)]
        W13 = [part(w, 0, 2, KD, FE) for w in w13]
        W2 = [part(w, 0, 4, D) for w in w2]
        dbuf = sb("dbuf", [P, 16384])

        x_tok = sb("x_tok", [P, 3, D])
        xT = sb("xT", [P, KD, T])
        ln_g = sb("ln_g", [P, D])
        ln_b = sb("ln_b", [P, D])
        ident = sb("ident", [P, P])
        ones = sb("ones", [P, P])
        before = sb("before", [P, P])
        eps = sb("eps", [P, 1])
        spare2 = sb("spare2", [1, 2])
        spare = sb("spare", [1, 4])
        vec_T = sb("vec_T", [P, 48])
        dw_T = sb("dw_T", [P, KD, CW])
        rw = sb("rw", [P, KD, E])
        rb = sb("rb", [P, 3, E])
        route = sb("route", [P, 3, 3 * E])
        bn = sb("bn", [P, 3, 2, 6])
        mv = sb("mv", [P, 3, 2])
        rstd = sb("rstd", [P, 3, 1])
        tok_id = sb("tok_id", [P, 3], I32)
        zeros_i = sb("zeros_i", [C, SLOTS], I32)
        idx = sb("idx", [C, SLOTS], I32)
        idx_col = [sb(f"idx_col{s}", [C, 1], I32) for s in range(3)]
        rounds = sb("rounds", [1, 4, E], I32)
        pos_i = sb("pos_i", [P, 2, 2, 3], I32)
        gates = sb("gates", [P, 2, 3])
        total_rounds = sb("total_rounds", [P, 1])
        ukT = sb("ukT", [P, NH, KV])

        B = [ctx.enter_context(nc.psum_tensor(f"bank{i}", [P, 512], F32))[:, :] for i in range(2)]
        wide = ctx.enter_context(nc.psum_tensor("wide", [P, 1024], F32))
        B += [wide[:, 0:512], wide[:, 512:1024]]
        B += [ctx.enter_context(nc.psum_tensor(f"bank{i}", [P, 512], F32))[:, :] for i in range(4, 8)]

        pw1 = [part(dbuf, s * 2048, KD, 2, P) for s in range(2)]
        pw2 = part(dbuf, 4096, KD, D)
        b_out = part(dbuf, 12288, D)
        dw_rows = part(dbuf, 13312, D)
        vec_rows = part(dbuf, 14336, P)
        mean_c = part(dbuf, 14464, T)
        rstd_c = part(dbuf, 14784, T)
        EXT = EXTP + DB * EXTS
        ext = part(w13[1], 0, KD, EXT)
        acc = part(w13[1], KD * EXT, KD, T)
        sq = [part(w2[1], 2048 + s * T, T) for s in range(2)]
        state = part(w2[1], 0, 2, D)
        sig = [part(w2[1], 2048 + (2 + s) * T, T) for s in range(2)]
        s_ext = part(dbuf, 15104, 2, DB, EXTS)
        s_w = part(dbuf, 15712, 2, 32)
        s_acc = part(dbuf, 15776, 2, DB, DS)
        s_term = [part(dbuf, 15904 + n * 128, 2, DB, DS) for n in range(3)]
        u_last = state
        zeros = part(w13[1], KD * (EXT + T), 512)
        u_samp = part(w2[1], 3328, KD, NS)

        M0 = 6656
        xg = [part(dbuf, M0 + s * 1024, D) for s in range(2)]
        xg_more = part(dbuf, M0 + 2048, D)
        xe = [part(dbuf, M0 + 3072 + s * 512, KD, C) for s in range(2)]
        xe_more = part(dbuf, M0 + 4096, KD, C)
        act_b = part(dbuf, M0 + 4608, FE)
        hid = part(dbuf, M0 + 5120, FE)
        act_more = part(dbuf, M0 + 5632, FE)
        hid_more = part(dbuf, M0 + 6144, FE)
        hT = [part(dbuf, M0 + 6656 + s * 256, 4, C) for s in range(2)]
        hT_more = part(dbuf, M0 + 7168, 4, C)
        ys = [part(dbuf, M0 + 7424 + s * 512, FE) for s in range(2)]
        ys_more = part(dbuf, M0 + 8448, FE)
        y_tok = part(dbuf, M0, 3, 2, D)
        lgT = part(dbuf, M0 + 3072, T)
        R0 = M0 + 3072 + T
        rt = [part(dbuf, R0 + 48 * n, 3, E) for n in range(14)]
        rs = part(dbuf, R0 + 48 * 14, 64)

        wdq = part(dbuf, 0, KD, QR)
        wkv = part(dbuf, 4096, KD, KV + ROPE)
        wuq = part(dbuf, 6656, 4, NH * (NOPE + ROPE))
        wuk = part(dbuf, 12800, 2, NH * NOPE)
        r1 = w13[1]
        q_peT = part(r1, 0, 4, T)
        qT = part(r1, 1280, NH, T)
        kT = part(r1, 3840, 2, T)
        kpeT = part(r1, 4480, T)
        ckv_tok = part(r1, 4800, 3, KV)
        kpe_tok = part(r1, 5568, 3, 2 * ROPE)
        cqT = part(r1, 5952, 4, T)
        r2 = w2[1]
        q_lat = [part(r2, s * 640, 2, T) for s in range(2)]
        q_stage = part(r2, 1280, 3, 4, 2 * NS)
        rope_T = part(dbuf, 14848, 2, T)
        swap = part(r2, 2816, P)
        rope_tok = part(r2, 2944, 3, 2, HALF)
        rq = part(r2, 3136, T)
        sqq = [part(r1, 7232 + s * T, T) for s in range(2)]
        q_tmp = sqq[0]
        gkv = part(r2, 3776, KV)
        sc = [part(r1, 7232 + s * 384, 384) for s in range(2)]
        pT = sb("pT", [P, 384])
        causal = sb("causal", [P, 384])
        sm = sb("sm", [P, 2, 8])
        olT = part(dbuf, 0, 2, NH, T)
        cache = [part(w13[0], s * 2 * NPG * KV, 2 * NPG, KV) for s in range(2)]
        cpe = [part(w2[0], s * 2 * NPG * ROPE, 2 * NPG, ROPE) for s in range(2)]
        KPs = part(w2[0], 2048, 2, PAST)
        k0, k1, k2 = (part(dbuf, 13312 + n * PAST, PAST) for n in range(3))
        KTs = [[k0, k1], [k2, part(r2, 0, PAST)]]
        probs = part(r2, 2816, PAST)
        own = part(r1, 7232, 4, NS)
        probs_new = part(r1, 7488, NS)
        pTs = part(r1, 5952, NPG, P)
        pTn = part(r1, 6976, P)
        ols = part(r1, 7552, KV)
        kss = sb("kss", [P, 2, 3])
        k_tmp = sb("k_tmp", [P, 2, HALF])
        rms_eps = sb("rms_eps", [P, 1])
        wuv = part(r1, 1280, 2, NH * VH)
        oT = xT
        wo = part(dbuf, 5120, KD, D)
        pages = sb("pages", [1, DB * NPG], I32)

        ld_x, ld_vec, ld_dw, ld_state, ld_misc = (sem(n) for n in ("ld_x", "ld_vec", "ld_dw", "ld_state", "ld_misc"))
        pw1_ready = [sem("pw1_ready0"), sem("pw1_ready1")]
        pw2_ready, ln_ready = sem("pw2_ready"), sem("ln_ready")
        ones_set, pad_set, ids_set, table_zero, x_scaled = (
            sem(n) for n in ("ones_set", "pad_set", "ids_set", "table_zero", "x_scaled"))
        xT_turned, xT_copied = sem("xT_turned"), sem("xT_copied")
        par_turned, glu_done, h_done, sig_done, tap = (
            sem(n) for n in ("par_turned", "glu_done", "h_done", "sig_done", "tap"))
        sum_done, cen_done, sq_done, sq_used, var_done, var_eps, rstd_done, nrm_done, z_done = (
            sem(n) for n in ("sum_done", "cen_done", "sq_done", "sq_used", "var_done", "var_eps", "rstd_done",
                             "nrm_done", "z_done"))
        mean_done, s_tap = sem("mean_done"), sem("s_tap")
        mix_done, mix_added = sem("mix_done"), sem("mix_added")
        u_packed = sem("u_packed")
        u_turned, u_copied, u_stored = sem("u_turned"), sem("u_copied"), sem("u_stored")
        dve_seq = sem("dve_seq")
        var_ready, rstd_ready, ln_done, x_stored = (sem(n) for n in ("var_ready", "rstd_ready", "ln_done", "x_stored"))
        r_logit, r_logit_c, r_turned, r_aff, r_mask, r_rank, r_pos, scattered, idx_ready = (
            sem(n) for n in ("r_logit", "r_logit_c", "r_turned", "r_aff", "r_mask", "r_rank", "r_pos", "scattered",
                             "idx_ready"))
        w13_ready, w2_ready = [sem("w13_ready0"), sem("w13_ready1")], [sem("w2_ready0"), sem("w2_ready1")]
        w13_free = sem("w13_free")
        idx_set = sem("idx_set")
        xg_ready, y_stored = [sem("xg_ready0"), sem("xg_ready1")], [sem("y_stored0"), sem("y_stored1")]
        xe_turned, xe_copied, up_done, act_done, hid_done, ht_turned, ht_copied, down_done, y_copied = (
            sem(n) for n in ("xe_turned", "xe_copied", "up_done", "act_done", "hid_done", "ht_turned", "ht_copied",
                             "down_done", "y_copied"))
        m_idx, m_xg, m_turned, m_copied, m_up, m_act, m_hid, m_ht, m_htc, m_down, m_y, m_stored = (
            sem("more_" + n) for n in ("idx", "xg", "turned", "copied", "up", "act", "hid", "ht", "htc", "down", "y",
                                       "stored"))
        y_zeroed = sem("y_zeroed")
        y_back, y_added = [sem(f"y_back{i}") for i in range(3)], sem("y_added")
        r_aff0, cnt_set = sem("r_aff0"), sem("cnt_set")
        ld_q, ld_kv, ld_uq, ld_uk, ld_uv, ld_o, ld_att = (
            sem(n) for n in ("ld_q", "ld_kv", "ld_uq", "ld_uk", "ld_uv", "ld_o", "ld_att"))
        out_stored = sem("out_stored")
        kv_done, kv_sq, kv_ready, kv_chain = (sem(n) for n in ("kv_done", "kv_sq", "kv_ready", "kv_chain"))
        cq_done, cq_copied, cq_sq_used, cq_var, cq_std, cq_ready = (
            sem(n) for n in ("cq_done", "cq_copied", "cq_sq_used", "cq_var", "cq_std", "cq_ready"))
        c_turned, kT_copied, q_done, qT_copied = (sem(n) for n in ("c_turned", "kT_copied", "q_done", "qT_copied"))
        qpe_done, qpe_raw, qpe_swapped, qpe_ready = (sem(n) for n in ("qpe_done", "qpe_raw", "qpe_swapped", "qpe_ready"))
        uk_turned, uk_copied, ql_done, ql_copied, staged, s_done, s_read, s_max, e_done, p_ready, p_turned, p_copied = (
            sem(n) for n in ("uk_turned", "uk_copied", "ql_done", "ql_copied", "staged", "s_done", "s_read", "s_max",
                             "e_done", "p_ready", "p_turned", "p_copied"))
        pv_done, ol_copied = sem("pv_done"), sem("ol_copied")
        pair_done, kt_turned, kt_a, kt_d, ss_done, ss_max, se_done, sp_turned, sp_a, sp_d = (
            sem(n) for n in ("pair_done", "kt_turned", "kt_a", "kt_d", "ss_done", "ss_max",
                             "se_done", "sp_turned", "sp_a", "sp_d"))
        ols_seq = sem("ols_seq")
        cache_ready = [sem("cache_ready0"), sem("cache_ready1")]
        cpe_ready = [sem("cpe_ready0"), sem("cpe_ready1")]
        ols_ready, ols_turned, ols_copied, uv_done, oT_copied, own_ready, pair_seq = (
            sem(n) for n in ("ols_ready", "ols_turned", "ols_copied", "uv_done", "oT_copied", "own_ready", "pair_seq"))

        ext_s = ext[:, :, EXTP:].rearrange("p k (b s) -> p k b s", b=DB)
        acc_s = acc[:, :, SEQ:].rearrange("p k (b s) -> p k b s", b=DB)

        def chunk(v, j, lo, n):
            return v[:, bass.ds(j, 1), lo:lo + n].rearrange("p o n -> p (o n)")

        def s_chunk(v, j, lo, n):
            return v[:, bass.ds(j, 1), :, lo:lo + n].rearrange("p o b n -> p (o b) n")

        def sp_program(sp):
            for n, (t0, m) in enumerate(TILES):
                src = a["x_prompt"][0, t0:t0 + m] if n < 2 else a["x_sample"].rearrange("b s d -> (b s) d")
                sp.dma_start(x_tok[0:m, n], src).then_inc(ld_x, 16)
            sp.dma_start(ident[:], a["c_ident"]).then_inc(ld_x, 16)
            w1v = a["a_w_pw1"][0].rearrange("(k p) (h c) -> p k h c", p=P, h=2)

            def load_pw1(j, s):
                for h in range(2):
                    sp.dma_start(pw1[s][:, :, h], w1v[:, :, h, bass.ts(j, P)]).then_inc(pw1_ready[s], 16)
            for s in range(2):
                load_pw1(s, s)
            with sp.Fori(0, 3) as it:
                for s in range(2):
                    sp.wait_ge(h_done, it * 2 + s + 1)
                    load_pw1(it * 2 + s + 2, s)
            sp.dma_start(pw2, a["a_w_pw2"][0].rearrange("(k p) n -> p k n", p=P)).then_inc(pw2_ready, 16)

            def load_13(l, e, s):
                for n, name in enumerate(("e_w1", "e_w3")):
                    src = a[name][l].rearrange("e (k p) f -> p e k f", p=P)[:, bass.ds(e, 1)]
                    sp.dma_start(W13[s][:, n], src.rearrange("p a k f -> p (a k) f")).then_inc(w13_ready[s], 16)

            def load_2(l, e, s):
                src = a["e_w2"][l].rearrange("e (k p) d -> p e k d", p=P)[:, bass.ds(e, 1)]
                sp.dma_start(W2[s], src.rearrange("p a k d -> p (a k) d")).then_inc(w2_ready[s], 16)

            def load_rest(l):
                with sp.Fori(0, (E - 2) // 2) as it:
                    for s in range(2):
                        e = it * 2 + s + 2
                        sp.wait_ge(w13_free, e + (E * l - 1))
                        load_13(l, e, s)
                        sp.wait_ge(down_done, e + (E * l - 1))
                        load_2(l, e, s)

            load_13(0, 0, 0)
            load_2(0, 0, 0)
            sp.wait_ge(mix_done, 3)
            sp.wait_ge(y_zeroed, 16 * ZEROED)
            sp.wait_ge(u_stored, 32)
            load_13(0, 1, 1)
            load_2(0, 1, 1)
            sp.dma_start(wdq, a["b_w_dq"][0].rearrange("(k p) n -> p k n", p=P)).then_inc(ld_q, 16)
            sp.dma_start(wkv[:, :, 0:KV], a["s_w_dkv"].rearrange("(k p) n -> p k n", p=P)).then_inc(ld_kv, 16)
            sp.dma_start(wkv[:, :, KV:], a["s_w_kr"].rearrange("(k p) n -> p k n", p=P)).then_inc(ld_kv, 16)
            load_rest(0)
            sp_attention(sp, load_13, load_2, load_rest)
            sp.wait_ge(out_stored, OUT_STORES * 16)

        def step(n):
            nc.gpsimd.tensor_tensor(spare[:, n:n + 1], spare[:, 0:1], spare[:, 0:1], ALU.mult)

        def pool_program(pool):
            nc.gpsimd.memset(eps[:], LN_EPS)
            nc.gpsimd.memset(rms_eps[:], RMS_EPS)
            nc.gpsimd.memset(spare[:], 0.0)
            nc.gpsimd.memset(ones[:], 1.0).then_inc(ones_set, 1)
            nc.gpsimd.memset(zeros_i[:], 0).then_inc(ids_set, 1)
            nc.gpsimd.iota(tok_id[:], pattern=[[P, 3]], base=0, channel_multiplier=1).then_inc(ids_set, 1)
            nc.gpsimd.memset(ext[:, :, 0:CS], 0.0).then_inc(pad_set, 1)
            nc.gpsimd.memset(zeros, 0.0).then_inc(pad_set, 1)
            pool.wait_ge(ids_set, 2)
            for l in range(DEPTH):
                pool.dma_start(slot_token[l].rearrange("(p s) o -> p (s o)", p=C), zeros_i[:]).then_inc(table_zero, 16)
            with pool.Fori(0, KD // 2) as it:
                for s in range(2):
                    j = it * 2 + s
                    at = bass.ds(j, 1)
                    pool.wait_ge(glu_done, j + 3)
                    nc.gpsimd.tensor_copy(s_ext[:, s], ext_s[:, at].rearrange("p o b n -> p (o b) n")).then_inc(s_tap, 1)
                    nc.gpsimd.tensor_copy(s_w[:, s, 0:CW], dw_T[:, at].rearrange("p o c -> p (o c)")).then_inc(s_tap, 1)
                    nc.gpsimd.tensor_copy(s_w[:, s, CW:CW + 1], vec_T[:, bass.ds(j + 16, 1)]).then_inc(s_tap, 1)

                def weight(k):
                    return s_w[:, :, k:k + 1].unsqueeze(3).to_broadcast([P, 2, DB, DS])

                pool.wait_ge(s_tap, it * S_TAPS + 6)
                for k in range(CW + 1):
                    if k < CW:
                        nc.gpsimd.tensor_tensor(s_term[k % 3], s_ext[:, :, :, k:k + DS], weight(k), ALU.mult)\
                            .then_inc(s_tap, 1)
                    if k >= 1:
                        pool.wait_ge(s_tap, it * S_TAPS + (2 * k + 5))
                        nc.gpsimd.tensor_tensor(s_acc, weight(CW) if k == 1 else s_acc, s_term[(k - 1) % 3], ALU.add)\
                            .then_inc(s_tap, 1)
                for s in range(2):
                    pool.wait_ge(s_tap, it * S_TAPS + (2 * CW + 6))
                    nc.gpsimd.tensor_copy(s_chunk(acc_s, it * 2 + s, 0, DS), s_acc[:, s]).then_inc(s_tap, 1)
            pool.wait_ge(pad_set, 2)
            for r in range(MORE * C // P):
                for h in range(2):
                    pool.dma_start(y_rows[E * C + r * P:E * C + (r + 1) * P, h * 512:(h + 1) * 512], zeros)\
                        .then_inc(y_zeroed, 16)
            pool.wait_ge(xT_turned, 6)
            pool.wait_ge(ld_misc, MISC)
            for n, (t0, m) in enumerate(TILES):
                nc.gpsimd.tensor_scalar(x_tok[0:m, n], x_tok[0:m, n], ALPHA, None, ALU.mult).then_inc(x_scaled, 1)
            for n, (t0, m) in enumerate(TILES):
                pool.wait_ge(x_scaled, n + 1)
                nc.gpsimd.tensor_tensor(x_tok[0:m, n], x_tok[0:m, n], b_out[0:m], ALU.add).then_inc(x_scaled, 1)
            pool.wait_ge(glu_done, KD + 2)
            nc.gpsimd.tensor_copy(u_samp.rearrange("p k (b s) -> p k b s", b=DB),
                                  ext[:, :, EXTP:].rearrange("p k (b s) -> p k b s", b=DB)[:, :, :, CS:EXTS])\
                .then_inc(u_packed, 1)
            pool_experts(pool, 0)
            for p in range(DB // 2):
                with pool.Fori(0, 2 * NPG // 4) as it:
                    page = [pool.value_load(pages[0:1, bass.ds(it * 4 + p * 2 * NPG + n, 1)], min_val=0,
                                            max_val=NPOOL - 1) for n in range(4)]
                    for n in range(4):
                        src = a["cache_kpe"][bass.ds(page[n], 1)].rearrange("o p r -> p (o r)")
                        if n == 0 and p >= 2:
                            pool.wait_ge(pair_done, p - 1)
                        elif n == 0:
                            pool.wait_ge(down_done, E - 1)
                        pool.dma_start(cpe[p % 2][:, bass.ds(it * 4 + n, 1)].rearrange("p o r -> p (o r)"), src)\
                            .then_inc(cpe_ready[p % 2], 16)
            pool_experts(pool, 1)

        def pool_experts(pool, l):
            pool.wait_ge(table_zero, 16 * DEPTH)
            pool.wait_ge(r_pos, l + 1)
            for k in range(2):
                for i, (t0, m) in enumerate(TILES):
                    nc.gpsimd.indirect_dma_start(
                        slot_token[l], bass.IndirectOffsetOnAxis(ap=pos_i[0:m, 0, k, i:i + 1], axis=0),
                        tok_id[0:m, i:i + 1], None).then_inc(scattered, 16)
            pool.wait_ge(scattered, 96 * (l + 1))
            pool.dma_start(idx[:], slot_token[l].rearrange("(p s) o -> p (s o)", p=C)).then_inc(idx_ready, 16)
            pool.wait_ge(idx_ready, 16 * (l + 1))
            pool.wait_ge(x_stored, 48 * (l + 1))
            pool.wait_ge(cnt_set, l + 1)

            def gather(e, s, g, more):
                nc.gpsimd.tensor_copy(idx_col[s][:], idx[:, bass.ds(e * CHUNKS, 1)]).then_inc(idx_set, 1)
                pool.wait_ge(idx_set, g + 1)
                step(1)
                nc.gpsimd.indirect_dma_start(xg[s][0:C], None, x_rows[l],
                                             bass.IndirectOffsetOnAxis(ap=idx_col[s][:], axis=0))\
                    .then_inc(xg_ready[s], 16)

            def further(e):
                count = pool.value_load(rounds[0:1, 0, bass.ds(e, 1)], min_val=0, max_val=CHUNKS - 1)
                first = pool.value_load(rounds[0:1, 1, bass.ds(e, 1)], min_val=0, max_val=32)
                with pool.If(count > 0):
                    with pool.Fori(1, count + 1) as c:
                        pool.wait_ge(m_stored, (first + c) * 32)
                        nc.gpsimd.tensor_copy(idx_col[2][:], idx[:, bass.ds(e * CHUNKS + c, 1)]).then_inc(m_idx, 1)
                        pool.wait_ge(m_idx, first + c)
                        step(2)
                        nc.gpsimd.indirect_dma_start(xg_more[0:C], None, x_rows[l],
                                                     bass.IndirectOffsetOnAxis(ap=idx_col[2][:], axis=0))\
                            .then_inc(m_xg, 16)
                with pool.Else():
                    pass

            g0 = E * l
            gather(0, 0, g0, False)
            gather(1, 1, g0 + 1, False)
            further(0)
            with pool.Fori(0, (E - 2) // 2) as it:
                for s in range(2):
                    e = it * 2 + s + 2
                    pool.wait_ge(xe_turned, e + (g0 - 1))
                    gather(e, s, e + g0, True)
                    further(e - 1)
            further(E - 1)
            pool.wait_ge(y_zeroed, 16 * ZEROED)
            last = pool.value_load(rounds[0:1, 2, 0:1], min_val=1, max_val=32)
            pool.wait_ge(y_stored[0], 16 * E * (l + 1))
            pool.wait_ge(y_stored[1], 16 * E * (l + 1) + 32)
            pool.wait_ge(m_stored, last * 32)
            step(3)
            pool.wait_ge(y_copied, E * (l + 1))
            for i, (t0, m) in enumerate(TILES):
                for k in range(2):
                    nc.gpsimd.indirect_dma_start(y_tok[0:m, i, k], None, y_rows,
                                                 bass.IndirectOffsetOnAxis(ap=pos_i[0:m, 1, k, i:i + 1], axis=0))\
                        .then_inc(y_back[i], 16)

        def act_program(act):
            for j, (name, n) in enumerate(VECS):
                r0 = sum(c for _, c in VECS[:j])
                act.dma_start(vec_rows[r0:r0 + n], a[name][0].rearrange("(r c) -> r c", c=P)).then_inc(ld_vec, 16)
            act.dma_start(dw_rows[0:CW], a["a_w_dw"][0]).then_inc(ld_dw, 16)
            for h in range(2):
                act.dma_start(state[0:4 * CS, h],
                              a["state_conv"][0, 4 * h:4 * h + 4].rearrange("b s d -> (b s) d")).then_inc(ld_state, 16)
            act.dma_start(b_out, a["a_b_pw2"].broadcast_to([P, D])).then_inc(ld_misc, 16)
            act.dma_start(before[:], a["c_before"]).then_inc(ld_misc, 16)
            act.dma_start(route[:], a["c_route"]).then_inc(ld_misc, 16)
            act.dma_start(rw[:], a["r_w"].rearrange("(k p) e -> p k e", p=P)).then_inc(ld_misc, 16)
            act.dma_start(pages[:], a["page_table"].rearrange("(o b) n -> o (b n)", o=1)).then_inc(ld_misc, 16)
            act.dma_start(causal[:], a["c_causal"]).then_inc(ld_misc, 16)
            for i in range(3):
                act.dma_start(rb[:, i], a["r_b"].unsqueeze(0).broadcast_to([P, E])).then_inc(ld_misc, 16)
            for h in range(2):
                act.dma_start(credit[h:h + 1], a["c_ident"][0:1]).then_inc(m_stored, 16)
                act.dma_start(credit[h + 2:h + 3], a["c_ident"][0:1]).then_inc(y_stored[1], 16)
            load_norm(act, 0)
            act.wait_ge(ones_set, 1)
            act.dma_start(a["conv_sample"][0, :, 0:CS - DS], a["state_conv"][0, :, DS:CS]).then_inc(out_stored, 16)
            copy_xT(act, 0)
            with act.Fori(0, KD // 2) as it:
                for s in range(2):
                    j = it * 2 + s
                    act.wait_ge(par_turned, 1)
                    act.wait_ge(h_done, j + 1)
                    act.wait_ge(glu_done, j + 1)
                    nc.scalar.activation(sig[s], B[2 * s + 1][:, 0:T], ACT.Sigmoid,
                                         bias=vec_T[:, bass.ds(j + KD, 1)]).then_inc(sig_done, 1)
            for j in range(KD):
                act.wait_ge(cen_done, j + 1)
                if j >= 2:
                    act.wait_ge(sq_used, j - 1)
                nc.scalar.activation(sq[j % 2], acc[:, j], ACT.Square).then_inc(sq_done, 1)
            act.wait_ge(var_eps, 1)
            nc.scalar.activation(rstd_c, rstd_c, ACT.Sqrt).then_inc(rstd_done, 1)
            for j in range(KD):
                act.wait_ge(nrm_done, j + 1)
                nc.scalar.activation(acc[:, j], acc[:, j], ACT.Silu, scale=vec_T[:, 24 + j:25 + j],
                                     bias=vec_T[:, 32 + j:33 + j]).then_inc(z_done, 1)
            act_norm(act, 0)
            for q in range(2):
                act.wait_ge(u_turned, q + 1)
                nc.scalar.activation(u_last[0:CS, 0, 512 * q:512 * q + 512], B[UB[q]][0:CS, :], ACT.Copy)\
                    .then_inc(u_copied, 1)
            for q in range(2):
                act.wait_ge(u_turned, q + 3)
                nc.scalar.activation(u_last[0:NS, 1, 512 * q:512 * q + 512], B[UB[q + 2]][0:NS, :], ACT.Copy)\
                    .then_inc(u_copied, 1)
            act.wait_ge(u_copied, 4)
            act.dma_start(a["conv_prompt"][0, 0], u_last[0:CS, 0]).then_inc(u_stored, 16)
            act.dma_start(a["conv_sample"][0, :, CS - DS:CS].rearrange("b s d -> b s d"), u_last[0:NS, 1])\
                .then_inc(u_stored, 16)
            act_experts(act, 0)
            act_attention(act)
            act_experts(act, 1)
            act.wait_ge(ln_done, 12)
            for i, (t0, m) in enumerate(TILES):
                dst = a["y_prompt"][0, t0:t0 + m] if i < 2 else a["y_sample"].rearrange("b s d -> (b s) d")
                act.dma_start(dst, x_tok[0:m, i]).then_inc(out_stored, 16)

        def act_norm(act, n):
            for i, (t0, m) in enumerate(TILES):
                act.wait_ge(var_ready, 3 * n + i + 1)
                nc.scalar.activation(rstd[0:m, i], mv[0:m, i, 1:2], ACT.Sqrt, bias=eps[0:m]).then_inc(rstd_ready, 1)

        def load_norm(act, n):
            if n:
                act.wait_ge(ln_done, 3 * n)
            g, b = ("ln_mix_g", "ln_mix_b") if n % 2 == 0 else ("ln_ffn_g", "ln_ffn_b")
            act.dma_start(ln_g[:], a[g][n // 2:n // 2 + 1].broadcast_to([P, D])).then_inc(ln_ready, 16)
            act.dma_start(ln_b[:], a[b][n // 2:n // 2 + 1].broadcast_to([P, D])).then_inc(ln_ready, 16)

        def copy_xT(act, r):
            for n in range(6):
                i, q = divmod(n, 2)
                t0, m = TILES[i]
                act.wait_ge(xT_turned, 6 * r + n + 1)
                src = B[n % 2][:, 0:4 * m].rearrange("p (k t) -> p k t", k=4)
                nc.scalar.activation(xT[:, 4 * q:4 * q + 4, t0:t0 + m], src, ACT.Copy).then_inc(xT_copied, 1)

        def act_experts(act, l):
            for i, (t0, m) in enumerate(TILES):
                act.wait_ge(ln_done, 6 * l + i + 1)
                act.dma_start(x_rows[l][t0:t0 + m], x_tok[0:m, i]).then_inc(x_stored, 16)
            load_norm(act, 2 * l + 1)
            copy_xT(act, 2 * l + 1)
            act.wait_ge(r_turned, l + 1)
            act.wait_ge(r_aff0, l + 1)
            nc.scalar.activation(rt[0][:, 0:2], B[3][:, 0:2 * E].rearrange("p (i e) -> p i e", i=2), ACT.Sigmoid)\
                .then_inc(r_aff, 1)
            nc.scalar.activation(rt[0][0:NS, 2], B[3][0:NS, 2 * E:3 * E], ACT.Sigmoid).then_inc(r_aff, 1)
            act.wait_ge(cnt_set, l + 1)
            act.wait_ge(y_zeroed, 16 * ZEROED)
            g0 = E * l

            def xe_copy(g, s):
                act.wait_ge(xe_turned, g + 1)
                nc.scalar.activation(xe[s], B[0][:, :].rearrange("p (k t) -> p k t", k=KD), ACT.Copy)\
                    .then_inc(xe_copied, 1)

            def silu(g, s, first=False):
                act.wait_ge(up_done, g + 1)
                if not first:
                    act.wait_ge(hid_done, g)
                nc.scalar.activation(act_b[0:C], B[1 + s][0:C], ACT.Silu).then_inc(act_done, 1)

            def store(e, g, s):
                act.wait_ge(y_copied, g + 1)
                for h in range(2):
                    act.dma_start(y_rows[bass.ds(e * C, C), h * FE:(h + 1) * FE], ys[s][h * C:(h + 1) * C])\
                        .then_inc(y_stored[s], 16)

            def further(e):
                count = act.value_load(rounds[0:1, 0, bass.ds(e, 1)], min_val=0, max_val=CHUNKS - 1)
                first = act.value_load(rounds[0:1, 1, bass.ds(e, 1)], min_val=0, max_val=32)
                row = act.value_load(rounds[0:1, 3, bass.ds(e, 1)], min_val=(E - 1) * C, max_val=(E + MORE - 6) * C)
                with act.If(count > 0):
                    with act.Fori(1, count + 1) as c:
                        act.wait_ge(m_turned, first + c)
                        nc.scalar.activation(xe_more, B[6][:, :].rearrange("p (k t) -> p k t", k=KD), ACT.Copy)\
                            .then_inc(m_copied, 1)
                        act.wait_ge(m_up, first + c)
                        nc.scalar.activation(act_more[0:C], B[7][0:C], ACT.Silu).then_inc(m_act, 1)
                        act.wait_ge(m_y, first + c)
                        for h in range(2):
                            act.dma_start(y_rows[bass.ds(row + c * C, C), h * FE:(h + 1) * FE],
                                          ys_more[h * C:(h + 1) * C]).then_inc(m_stored, 16)
                with act.Else():
                    pass

            xe_copy(g0, 0)
            silu(g0, 0, l == 0)
            xe_copy(g0 + 1, 1)
            further(0)
            silu(g0 + 1, 1)
            xe_copy(g0 + 2, 0)
            store(0, g0, 0)
            further(1)
            with act.Fori(0, (E - 4) // 2) as it:
                for s in range(2):
                    e = it * 2 + s + 2
                    silu(e + g0, s)
                    xe_copy(e + (g0 + 1), 1 - s)
                    store(e - 1, e + (g0 - 1), 1 - s)
                    further(e)
            silu(g0 + E - 2, 0)
            xe_copy(g0 + E - 1, 1)
            store(E - 3, g0 + E - 3, 1)
            further(E - 2)
            silu(g0 + E - 1, 1)
            store(E - 2, g0 + E - 2, 0)
            further(E - 1)
            store(E - 1, g0 + E - 1, 1)
            act_norm(act, 2 * l + 1)

        def pe_program(pe):
            pe.wait_ge(ld_x, 64)
            turn_x(pe, 0, 0)
            pe.wait_ge(ld_vec, 16 * len(VECS))
            pe.wait_ge(ld_dw, 16)
            nc.tensor.transpose(B[2][:, 0:NVEC], vec_rows[0:NVEC], ident[0:NVEC, 0:NVEC])
            for k in range(KD):
                last = nc.tensor.transpose(B[2][:, 64 + k * CW:64 + (k + 1) * CW], dw_rows[0:CW, k * P:(k + 1) * P],
                                           ident[0:CW, 0:CW])
            last.then_inc(par_turned, 1)
            pe.wait_ge(ld_state, 32)
            for h in range(2):
                for q in range(2):
                    for k in range(4):
                        last = nc.tensor.transpose(B[4 + 2 * h + q][:, k * 4 * CS:(k + 1) * 4 * CS],
                                                   state[0:4 * CS, h, (4 * q + k) * P:(4 * q + k + 1) * P],
                                                   ident[0:4 * CS, 0:4 * CS])
                    last.then_inc(par_turned, 1)
            pe.wait_ge(xT_copied, 6)
            pe.wait_ge(ones_set, 1)

            def gated(it):
                for s in range(2):
                    pe.wait_ge(pw1_ready[s], (it + 1) * 32)
                    pe.wait_ge(glu_done, it * 2 + (s + 1))
                    for h in range(2):
                        for k in range(KD):
                            last = nc.tensor.matmul(B[2 * s + h][:, 0:T], pw1[s][:, k, h], xT[:, k], start=(k == 0),
                                                    stop=(k == KD - 1))
                    last.then_inc(h_done, 1)

            def add_channels(it, start, stop):
                pe.wait_ge(tap, (it + 1) * TAPS)
                pe.wait_ge(s_tap, (it + 1) * S_TAPS)
                for s in range(2):
                    last = nc.tensor.matmul(B[4][:, 0:T], ones[:], chunk(acc, it * 2 + s, 0, T),
                                            start=start and s == 0, stop=stop and s == 1)
                return last

            gated(0)
            gated(1)
            pe.wait_ge(glu_done, 2)
            add_channels(0, True, False)
            with pe.Fori(2, KD // 2) as it:
                gated(it)
                add_channels(it - 1, False, False)
            add_channels(KD // 2 - 1, False, True).then_inc(sum_done, 1)
            for j in range(KD):
                pe.wait_ge(sq_done, j + 1)
                nc.tensor.matmul(B[5][:, 0:T], ones[:], sq[j % 2], start=(j == 0), stop=(j == KD - 1))\
                    .then_inc(sq_used, 1)
            pe.wait_ge(pw2_ready, 16)
            out_product(pe, acc, pw2, z_done, 8)
            for q in range(2):
                for k in range(4):
                    last = nc.tensor.transpose(B[UB[q]][0:CS, k * P:(k + 1) * P], ext[:, 4 * q + k, SEQ:EXTP],
                                               ident[:])
                last.then_inc(u_turned, 1)
            for q in range(2):
                if q == 0:
                    pe.wait_ge(u_packed, 1)
                else:
                    pe.wait_ge(u_copied, 1)
                for k in range(4):
                    last = nc.tensor.transpose(B[UB[q + 2]][0:NS, k * P:(k + 1) * P],
                                               u_samp[:, 4 * q + k], ident[:])
                last.then_inc(u_turned, 1)
            pe_experts(pe, 0)
            pe_attention(pe)
            pe_experts(pe, 1)

        def turn_x(pe, r, n0):
            for n in range(6):
                i, q = divmod(n, 2)
                t0, m = TILES[i]
                if r:
                    pe.wait_ge(ln_done, 3 * n0 + i + 1)
                if r or n >= 2:
                    pe.wait_ge(xT_copied, 6 * r + n - 1)
                for k in range(4):
                    last = nc.tensor.transpose(B[n % 2][:, k * m:(k + 1) * m],
                                               x_tok[0:m, i, (4 * q + k) * P:(4 * q + k + 1) * P], ident[0:m, 0:m])
                last.then_inc(xT_turned, 1)

        def out_product(pe, left, w, ready, n_ready):
            for i, (t0, m) in enumerate(TILES):
                for k in range(KD):
                    if i == 0:
                        pe.wait_ge(ready, n_ready - KD + k + 1)
                    for h in range(2):
                        dst = B[2 * i + h] if i < 2 else B[6][h * C:(h + 1) * C]
                        last = nc.tensor.matmul(dst, left[:, k, t0:t0 + m], w[:, k, h * 512:(h + 1) * 512],
                                                start=(k == 0), stop=(k == KD - 1))
                last.then_inc(mix_done, 1)

        def pe_experts(pe, l):
            turn_x(pe, 2 * l + 1, 2 * l)
            pe.wait_ge(ld_misc, MISC)
            pe.wait_ge(xT_copied, 6 * (2 * l + 2))
            for k in range(KD):
                last = nc.tensor.matmul(B[2][0:E, 0:T], rw[:, k], xT[:, k], start=(k == 0), stop=(k == KD - 1))
            last.then_inc(r_logit, 1)
            pe.wait_ge(r_logit_c, l + 1)
            for i, (t0, m) in enumerate(TILES):
                last = nc.tensor.transpose(B[3][0:m, i * E:(i + 1) * E], lgT[0:E, t0:t0 + m], ident[0:E, 0:E])
            last.then_inc(r_turned, 1)
            pe.wait_ge(r_mask, l + 1)
            mask = rt[MASK]
            for i, (t0, m) in enumerate(TILES):
                for n in range(i + 1):
                    mm = TILES[n][1]
                    left = before[0:mm, 0:m] if n == i else ones[0:mm, 0:m]
                    last = nc.tensor.matmul(B[6][0:m, i * E:(i + 1) * E], left, mask[0:mm, n], start=(n == 0),
                                            stop=(n == i))
            for n, (t0, m) in enumerate(TILES):
                last = nc.tensor.matmul(B[6][:, 3 * E:4 * E], ones[0:m, :], mask[0:m, n], start=(n == 0),
                                        stop=(n == 2))
            last.then_inc(r_rank, 1)
            pe.wait_ge(cnt_set, l + 1)
            g0 = E * l

            def turn_rows(bank, src, n):
                for k in range(n):
                    last = nc.tensor.matmul(bank[:, k * C:(k + 1) * C], src[0:C, k * P:(k + 1) * P], ident[0:C, 0:C],
                                            start=True, stop=True, is_transpose=k > 0)
                return last

            def turn(g, s):
                pe.wait_ge(xg_ready[s], (g // 2 + 1) * 16 if isinstance(g, int) else g)
                turn_rows(B[0], xg[s], KD).then_inc(xe_turned, 1)

            def up(x, bank, w, free):
                for k in range(KD):
                    for n in range(2):
                        last = nc.tensor.matmul(bank[n * C:(n + 1) * C], x[:, k], w[:, n, k], start=(k == 0),
                                                stop=(k == KD - 1))
                        if free and k == 0 and n == 0:
                            last.then_inc(w13_free, 1)
                return last

            def down(h, bank, w):
                for k in range(4):
                    for n in range(2):
                        last = nc.tensor.matmul(bank[n * C:(n + 1) * C], h[:, k], w[:, k, n * 512:(n + 1) * 512],
                                                start=(k == 0), stop=(k == 3))
                return last

            def do_up(g, s, n13):
                pe.wait_ge(w13_ready[s], n13)
                pe.wait_ge(xe_copied, g + 1)
                if not (isinstance(g, int) and g < 2):
                    pe.wait_ge(hid_done, g - 1)
                up(xe[s], B[1 + s], W13[s], not (isinstance(g, int) and g == 0)).then_inc(up_done, 1)

            def do_down(g, s, n2):
                pe.wait_ge(w2_ready[s], n2)
                pe.wait_ge(ht_copied, g + 1)
                if not (isinstance(g, int) and g < 2):
                    pe.wait_ge(y_copied, g - 1)
                down(hT[s], B[4 + s], W2[s]).then_inc(down_done, 1)

            def do_hidden(g, s):
                pe.wait_ge(hid_done, g + 1)
                if not (isinstance(g, int) and g < 1):
                    pe.wait_ge(ht_copied, g)
                turn_rows(B[3], hid, 4).then_inc(ht_turned, 1)

            def further(e, s, n2):
                count = pe.value_load(rounds[0:1, 0, bass.ds(e, 1)], min_val=0, max_val=CHUNKS - 1)
                first = pe.value_load(rounds[0:1, 1, bass.ds(e, 1)], min_val=0, max_val=32)
                with pe.If(count > 0):
                    with pe.Fori(1, count + 1) as c:
                        pe.wait_ge(m_xg, (first + c) * 16)
                        turn_rows(B[6], xg_more, KD).then_inc(m_turned, 1)
                        pe.wait_ge(m_copied, first + c)
                        up(xe_more, B[7], W13[s], False).then_inc(m_up, 1)
                        pe.wait_ge(m_hid, first + c)
                        turn_rows(B[6], hid_more, 4).then_inc(m_ht, 1)
                        pe.wait_ge(m_htc, first + c)
                        pe.wait_ge(w2_ready[s], n2)
                        down(hT_more, B[7], W2[s]).then_inc(m_down, 1)
                with pe.Else():
                    pass

            n = 16 * (E // 2) * l
            turn(g0, 0)
            do_up(g0, 0, 2 * n + 32)
            turn(g0 + 1, 1)
            do_hidden(g0, 0)
            further(0, 0, n + 16)
            do_up(g0 + 1, 1, 2 * n + 32)
            turn(g0 + 2, 0)
            do_down(g0, 0, n + 16)
            do_hidden(g0 + 1, 1)
            further(1, 1, n + 16)
            with pe.Fori(0, (E - 4) // 2) as it:
                for s in range(2):
                    e = it * 2 + s + 2
                    do_up(e + g0, s, it * 32 + (2 * n + 64))
                    turn_next = it * 16 + (n + 32 + 16 * s)
                    pe.wait_ge(xg_ready[1 - s], turn_next)
                    turn_rows(B[0], xg[1 - s], KD).then_inc(xe_turned, 1)
                    do_down(e + (g0 - 1), 1 - s, it * 16 + (n + 16 + 16 * s))
                    do_hidden(e + g0, s)
                    further(e, s, it * 16 + (n + 32))
            do_up(g0 + E - 2, 0, 2 * n + 256)
            turn(g0 + E - 1, 1)
            do_down(g0 + E - 3, 1, n + 112)
            do_hidden(g0 + E - 2, 0)
            further(E - 2, 0, n + 128)
            do_up(g0 + E - 1, 1, 2 * n + 256)
            do_down(g0 + E - 2, 0, n + 128)
            do_hidden(g0 + E - 1, 1)
            further(E - 1, 1, n + 128)
            do_down(g0 + E - 1, 1, n + 128)

        def dve_program(dve):
            V = nc.vector
            seq = [0]

            def after(ins):
                seq[0] += 1
                ins.then_inc(dve_seq, 1)
                dve.wait_ge(dve_seq, seq[0])

            def mark(ins):
                seq[0] += 1
                ins.then_inc(dve_seq, 1)
                return seq[0]

            dve.wait_ge(par_turned, 1)
            V.tensor_copy(vec_T[:, 0:NVEC], B[2][:, 0:NVEC])
            V.tensor_copy(dw_T[:, :, :], B[2][:, 64:64 + KD * CW].rearrange("p (k c) -> p k c", k=KD))\
                .then_inc(glu_done, 1)
            for h in range(2):
                for q in range(2):
                    dve.wait_ge(par_turned, 2 + 2 * h + q)
                    for k in range(4):
                        last = V.tensor_copy(ext_s[:, 4 * q + k, 4 * h:4 * h + 4, 0:CS],
                                             B[4 + 2 * h + q][:, k * 4 * CS:(k + 1) * 4 * CS]
                                             .rearrange("p (b s) -> p b s", b=4))
            last.then_inc(glu_done, 1)
            dve.wait_ge(pad_set, 1)
            with dve.Fori(0, KD // 2) as it:
                for s in range(2):
                    j = it * 2 + s
                    dve.wait_ge(sig_done, j + 1)
                    V.scalar_tensor_tensor(chunk(ext, j, CS, SEQ), B[2 * s][:, 0:SEQ], vec_T[:, bass.ds(j, 1)],
                                           sig[s][:, 0:SEQ], ALU.add, ALU.mult).then_inc(tap, 1)
                    V.scalar_tensor_tensor(s_chunk(ext_s, j, CS, DS),
                                           B[2 * s][:, SEQ:T].rearrange("p (b s) -> p b s", b=DB),
                                           vec_T[:, bass.ds(j, 1)], sig[s][:, SEQ:T].rearrange("p (b s) -> p b s", b=DB),
                                           ALU.add, ALU.mult).then_inc(glu_done, 1)
                for k in range(CW):
                    for s in range(2):
                        j = it * 2 + s
                        w = dw_T[:, bass.ds(j, 1), k:k + 1].rearrange("p o c -> p (o c)")
                        dve.wait_ge(tap, it * TAPS + (2 * k + s + 1))
                        if k == 0:
                            V.tensor_scalar(chunk(acc, j, 0, SEQ), chunk(ext, j, 0, SEQ), w,
                                            vec_T[:, bass.ds(j + 16, 1)], ALU.mult, ALU.add).then_inc(tap, 1)
                        else:
                            V.scalar_tensor_tensor(chunk(acc, j, 0, SEQ), chunk(ext, j, k, SEQ), w,
                                                   chunk(acc, j, 0, SEQ), ALU.mult, ALU.add).then_inc(tap, 1)
            dve.wait_ge(sum_done, 1)
            V.tensor_scalar(mean_c, B[4][:, 0:T], 1.0 / D, None, ALU.mult).then_inc(mean_done, 1)
            dve.wait_ge(mean_done, 1)
            for j in range(KD):
                V.tensor_tensor(acc[:, j], acc[:, j], mean_c, ALU.subtract).then_inc(cen_done, 1)
            dve.wait_ge(sq_used, KD)
            V.tensor_scalar(rstd_c, B[5][:, 0:T], 1.0 / D, LN_EPS, ALU.mult, ALU.add).then_inc(var_eps, 1)
            dve.wait_ge(rstd_done, 1)
            after(V.reciprocal(rstd_c, rstd_c))
            dve.wait_ge(cen_done, KD)
            for j in range(KD):
                V.tensor_tensor(acc[:, j], acc[:, j], rstd_c, ALU.mult).then_inc(nrm_done, 1)
            dve.wait_ge(x_scaled, 6)

            def norm(n):
                dve.wait_ge(ln_ready, 32 * (n + 1))
                for i, (t0, m) in enumerate(TILES):
                    dve.wait_ge(rstd_ready, 3 * n + i + 1)
                    V_x = x_tok[0:m, i]
                    after(V.reciprocal(rstd[0:m, i], rstd[0:m, i]))
                    after(V.tensor_scalar(V_x, V_x, mv[0:m, i, 0:1], rstd[0:m, i], ALU.subtract, ALU.mult))
                    after(V.tensor_tensor(V_x, V_x, ln_g[0:m], ALU.mult))
                    V.tensor_tensor(V_x, V_x, ln_b[0:m], ALU.add).then_inc(ln_done, 1)

            def stats(n, i, m):
                for h in range(2):
                    nxt = V.bn_stats(bn[0:m, i, h], x_tok[0:m, i, h * 512:(h + 1) * 512])
                    if h == 0:
                        mark(nxt)
                    else:
                        after(nxt)
                V.bn_aggr(mv[0:m, i], bn[0:m, i].rearrange("p a b -> p (a b)")).then_inc(var_ready, 1)

            def mix_norm(n, alpha):
                for i, (t0, m) in enumerate(TILES):
                    dve.wait_ge(mix_done, 3 * (n // 2) + i + 1)
                    for h in range(2):
                        src = B[2 * i + h][:, :] if i < 2 else B[6][h * C:(h + 1) * C, :]
                        V_x = x_tok[0:m, i, h * 512:(h + 1) * 512]
                        nxt = V.scalar_tensor_tensor(V_x, V_x, alpha, src, ALU.mult, ALU.add)
                        mark(nxt)
                    dve.wait_ge(dve_seq, seq[0])
                    stats(n, i, m)
                norm(n)

            mix_norm(0, 1.0)
            dve_experts(dve, 0, after, mark, stats, norm)
            dve_attention(dve, after, mark, seq)
            mix_norm(2, ALPHA)
            dve_experts(dve, 1, after, mark, stats, norm)

        def dve_experts(dve, l, after, mark, stats, norm):
            V = nc.vector
            aff, sel, pm, pn, gs, w16, oh1, oh2, t1, t2, masked, eq, first, mask = rt
            dve.wait_ge(r_logit, l + 1)
            V.memset(aff, 1.0).then_inc(r_aff0, 1)
            V.tensor_copy(lgT[0:E], B[2][0:E, 0:T]).then_inc(r_logit_c, 1)
            dve.wait_ge(ld_misc, MISC)
            dve.wait_ge(r_aff, 2 * (l + 1))
            order = route[:, 0, :].rearrange("p (i e) -> p i e", i=3)
            after(V.tensor_tensor(sel, aff, rb[:], ALU.add))
            pairs = sel.rearrange("p i (g a b) -> p (i g) a b", g=NG, a=2)
            flat = lambda v, n: v.rearrange("p i e -> p (i e)")[:, 0:n]
            hi, lo = flat(pm, 24), flat(pn, 24)
            hi2, lo2 = (x.rearrange("p (g a) -> p g a", a=2) for x in (hi, lo))
            after(V.tensor_tensor(hi2, pairs[:, :, :, 0], pairs[:, :, :, 1], ALU.max))
            after(V.tensor_tensor(lo2, pairs[:, :, :, 0], pairs[:, :, :, 1], ALU.min))
            a12, b12, g12 = flat(t1, 12), flat(t2, 12), flat(gs, 12)
            after(V.tensor_tensor(a12, hi2[:, :, 0], hi2[:, :, 1], ALU.min))
            after(V.tensor_tensor(b12, lo2[:, :, 0], lo2[:, :, 1], ALU.max))
            after(V.tensor_tensor(a12, a12, b12, ALU.max))
            after(V.tensor_tensor(b12, hi2[:, :, 0], hi2[:, :, 1], ALU.max))
            after(V.tensor_tensor(g12, a12, b12, ALU.add))
            g34 = g12.rearrange("p (i g) -> p i g", i=3)

            def first_best(values, n, tmp, out):
                r3 = flat(masked if n == NG else eq, 48)[:, 45:48]
                after(V.tensor_reduce(r3, values, AX.X, ALU.max))
                after(V.tensor_tensor(tmp, values, r3.unsqueeze(2).to_broadcast([P, 3, n]), ALU.is_equal))
                after(V.tensor_tensor(tmp, tmp, order[:, :, 0:n], ALU.mult))
                after(V.tensor_reduce(r3, tmp, AX.X, ALU.max))
                after(V.tensor_tensor(out, tmp, r3.unsqueeze(2).to_broadcast([P, 3, n]), ALU.is_equal))

            ohg = flat(w16, 12).rearrange("p (i g) -> p i g", i=3)
            first_best(g34, NG, a12.rearrange("p (i g) -> p i g", i=3), ohg)
            ohg12 = flat(w16, 12)
            pen = flat(t2, 12)
            after(V.tensor_scalar(pen, ohg12, BIG, -BIG, ALU.mult, ALU.add))
            m124 = masked.rearrange("p i (g b) -> p (i g) b", g=NG)
            s124 = sel.rearrange("p i (g b) -> p (i g) b", g=NG)
            after(V.tensor_tensor(m124, s124, ohg12.unsqueeze(2).to_broadcast([P, 12, EG]), ALU.mult))
            after(V.tensor_tensor(m124, m124, pen.unsqueeze(2).to_broadcast([P, 12, EG]), ALU.add))
            first_best(masked, E, first, oh1)
            after(V.scalar_tensor_tensor(masked, oh1, -BIG, masked, ALU.mult, ALU.add))
            first_best(masked, E, first, oh2)
            V.tensor_tensor(mask, oh1, oh2, ALU.add).then_inc(r_mask, 1)
            for k, oh in enumerate((oh1, oh2)):
                after(V.tensor_tensor(t1, oh, aff, ALU.mult))
                after(V.tensor_reduce(gates[:, k], t1, AX.X, ALU.add))
            total = flat(t2, 3)
            after(V.tensor_tensor(total, gates[:, 0], gates[:, 1], ALU.add))
            after(V.reciprocal(total, total))
            for k in range(2):
                after(V.tensor_tensor(gates[:, k], gates[:, k], total, ALU.mult))
            dve.wait_ge(r_rank, l + 1)
            rank = pm
            after(V.memset(rank, 0.0))
            after(V.tensor_copy(rank[:, 0:2], B[6][:, 0:2 * E].rearrange("p (i e) -> p i e", i=2)))
            after(V.tensor_copy(rank[0:NS, 2], B[6][0:NS, 2 * E:3 * E]))
            after(V.tensor_copy(rs[:, 48:64], B[6][:, 3 * E:4 * E]))
            cnt, n16, c16, d16 = rs[:, 48:64], first[:, 0], first[:, 1], first[:, 2]
            after(V.tensor_scalar(n16, cnt, float(C), None, ALU.is_gt))
            for c in range(2, CHUNKS):
                after(V.scalar_tensor_tensor(n16, cnt, float(c * C), n16, ALU.is_gt, ALU.add))
            after(V.tensor_copy(c16, n16))
            src, dst = c16, d16
            for step in (1, 2, 4, 8):
                after(V.tensor_copy(dst[:, 0:step], src[:, 0:step]))
                after(V.tensor_tensor(dst[:, step:E], src[:, step:E], src[:, 0:E - step], ALU.add))
                src, dst = dst, src
            after(V.tensor_tensor(dst, src, n16, ALU.subtract))
            for k, oh in enumerate((oh1, oh2)):
                for n, of in enumerate((rank, route[:, 1, :].rearrange("p (i e) -> p i e", i=3),
                                        dst.unsqueeze(1).to_broadcast([P, 3, E]))):
                    after(V.tensor_tensor(t1, oh, of, ALU.mult))
                    after(V.tensor_reduce(rs[:, 6 * n + 3 * k:6 * n + 3 * k + 3], t1, AX.X, ALU.add))
            r6, e6, m6, q6, p6, y6 = (rs[:, 6 * n:6 * n + 6] for n in range(6))
            after(V.tensor_scalar(q6, r6, float(C), None, ALU.is_ge))
            after(V.tensor_scalar(m6, m6, float(C), float((E - 1) * C), ALU.mult, ALU.add))
            after(V.scalar_tensor_tensor(m6, e6, -float(C) / CHUNKS, m6, ALU.mult, ALU.add))
            after(V.tensor_tensor(m6, m6, q6, ALU.mult))
            after(V.tensor_tensor(m6, m6, r6, ALU.add))
            after(V.scalar_tensor_tensor(y6, e6, float(C) / CHUNKS, m6, ALU.mult, ALU.add))
            after(V.tensor_scalar(y6, y6, 0.25, None, ALU.add))
            for c in range(2, CHUNKS):
                after(V.scalar_tensor_tensor(q6, r6, float(c * C), q6, ALU.is_ge, ALU.add))
            after(V.scalar_tensor_tensor(p6, r6, float(SLOTS), e6, ALU.mult, ALU.add))
            after(V.scalar_tensor_tensor(p6, q6, float(1 - C * SLOTS), p6, ALU.mult, ALU.add))
            after(V.tensor_copy(pos_i[:, 0].rearrange("p k i -> p (k i)"), p6))
            V.tensor_copy(pos_i[:, 1].rearrange("p k i -> p (k i)"), y6).then_inc(r_pos, 1)
            if l == 0:
                after(V.memset(total_rounds[:], 0.0))
            after(V.tensor_copy(rounds[0:1, 0], n16[0:1]))
            after(V.tensor_scalar(n16[0:1], dst[0:1], float(C), float((E - 1) * C), ALU.mult, ALU.add))
            after(V.tensor_copy(rounds[0:1, 3], n16[0:1]))
            after(V.tensor_scalar(dst, dst, total_rounds[:], None, ALU.add))
            after(V.tensor_copy(rounds[0:1, 1], dst[0:1]))
            after(V.tensor_tensor(total_rounds[:], total_rounds[:], src[:, E - 1:E], ALU.add))
            V.tensor_scalar(rounds[0:1, 2, 0:1], total_rounds[0:1], 1.0, None, ALU.add).then_inc(cnt_set, 1)
            dve.wait_ge(cnt_set, l + 1)
            g0 = E * l

            def gate_hidden(g, s):
                dve.wait_ge(act_done, g + 1)
                if not (isinstance(g, int) and g < 1):
                    dve.wait_ge(ht_turned, g)
                V.tensor_tensor(hid[0:C], act_b[0:C], B[1 + s][C:2 * C], ALU.mult).then_inc(hid_done, 1)

            def copy_y(g, s):
                dve.wait_ge(down_done, g + 1)
                if isinstance(g, int):
                    if g >= 2:
                        dve.wait_ge(y_stored[s], (g // 2) * 32 + 32 * s)
                V.tensor_copy(ys[s], B[4 + s][:, :]).then_inc(y_copied, 1)

            def copy_hidden(g, s):
                dve.wait_ge(ht_turned, g + 1)
                V.tensor_copy(hT[s], B[3][:, 0:4 * C].rearrange("p (k t) -> p k t", k=4)).then_inc(ht_copied, 1)

            def further(e):
                count = dve.value_load(rounds[0:1, 0, bass.ds(e, 1)], min_val=0, max_val=CHUNKS - 1)
                first_r = dve.value_load(rounds[0:1, 1, bass.ds(e, 1)], min_val=0, max_val=32)
                with dve.If(count > 0):
                    with dve.Fori(1, count + 1) as c:
                        dve.wait_ge(m_act, first_r + c)
                        V.tensor_tensor(hid_more[0:C], act_more[0:C], B[7][C:2 * C], ALU.mult).then_inc(m_hid, 1)
                        dve.wait_ge(m_ht, first_r + c)
                        V.tensor_copy(hT_more, B[6][:, 0:4 * C].rearrange("p (k t) -> p k t", k=4))\
                            .then_inc(m_htc, 1)
                        dve.wait_ge(m_down, first_r + c)
                        V.tensor_copy(ys_more, B[7][:, :]).then_inc(m_y, 1)
                with dve.Else():
                    pass

            gate_hidden(g0, 0)
            copy_hidden(g0, 0)
            further(0)
            gate_hidden(g0 + 1, 1)
            copy_y(g0, 0)
            copy_hidden(g0 + 1, 1)
            further(1)
            n = 16 * E * l
            with dve.Fori(0, (E - 4) // 2) as it:
                for s in range(2):
                    e = it * 2 + s + 2
                    gate_hidden(e + g0, s)
                    if s == 1:
                        dve.wait_ge(y_stored[0], it * 32 + (n + 32))
                    else:
                        dve.wait_ge(y_stored[1], it * 32 + (n + 32))
                    copy_y(e + (g0 - 1), 1 - s)
                    copy_hidden(e + g0, s)
                    further(e)
            gate_hidden(g0 + E - 2, 0)
            copy_y(g0 + E - 3, 1)
            copy_hidden(g0 + E - 2, 0)
            further(E - 2)
            gate_hidden(g0 + E - 1, 1)
            copy_y(g0 + E - 2, 0)
            copy_hidden(g0 + E - 1, 1)
            further(E - 1)
            copy_y(g0 + E - 1, 1)
            for i, (t0, m) in enumerate(TILES):
                V_x = x_tok[0:m, i]
                after(V.tensor_scalar(V_x, V_x, ALPHA, None, ALU.mult))
                dve.wait_ge(y_back[i], 32 * (l + 1))
                for k in range(2):
                    after(V.scalar_tensor_tensor(V_x, y_tok[0:m, i, k], gates[0:m, k, i:i + 1], V_x, ALU.mult, ALU.add))
                stats(2 * l + 1, i, m)
            norm(2 * l + 1)

        def sp_attention(sp, load_13, load_2, load_rest):
            def load_pair(p):
                with sp.Fori(0, 2 * NPG // 4) as it:
                    page = [sp.value_load(pages[0:1, bass.ds(it * 4 + p * 2 * NPG + n, 1)], min_val=0,
                                          max_val=NPOOL - 1) for n in range(4)]
                    for n in range(4):
                        src = a["cache_ckv"][bass.ds(page[n], 1)].rearrange("o p r -> p (o r)")
                        if n == 0 and p >= 2:
                            sp.wait_ge(pair_done, p - 1)
                        elif n == 0:
                            sp.wait_ge(down_done, E - 1)
                        sp.dma_start(cache[p % 2][:, bass.ds(it * 4 + n, 1)].rearrange("p o r -> p (o r)"), src)\
                            .then_inc(cache_ready[p % 2], 16)

            sp.wait_ge(ld_misc, MISC)
            load_pair(0)
            sp.wait_ge(var_ready, 6)
            sp.wait_ge(down_done, E)
            sp.dma_start(gkv, a["s_g_kv"].unsqueeze(0).broadcast_to([P, KV])).then_inc(ld_att, 16)
            sp.dma_start(rope_tok, a["c_rope_tok"]).then_inc(ld_att, 16)
            sp.dma_start(wuq, a["b_w_uq"][0].rearrange("(k p) h d -> p k (h d)", p=P)).then_inc(ld_uq, 16)
            sp.dma_start(rope_T, a["c_rope_T"]).then_inc(ld_att, 16)
            sp.dma_start(swap, a["c_swap"]).then_inc(ld_att, 16)
            sp.dma_start(wuk, a["s_w_uk"].rearrange("(c p) h d -> p c (h d)", p=P)).then_inc(ld_uk, 16)
            load_pair(1)
            sp.wait_ge(uk_turned, 4)
            sp.dma_start(wo, a["b_w_o"][0].rearrange("(k p) n -> p k n", p=P)).then_inc(ld_o, 16)
            load_pair(2)
            load_pair(3)
            sp.wait_ge(pair_done, DB // 2)
            load_13(1, 0, 0)
            load_2(1, 0, 0)
            sp.wait_ge(uv_done, NH)
            load_13(1, 1, 1)
            load_2(1, 1, 1)
            load_rest(1)

        def act_attention(act):
            load_norm(act, 2)
            copy_xT(act, 2)
            for i, (t0, m) in enumerate(TILES):
                act.wait_ge(kv_done, i + 1)
                nc.scalar.activation(ckv_tok[0:m, i], B[2 + i][0:m, 0:KV], ACT.Square,
                                     accum_out=kss[0:m, 0, i:i + 1]).then_inc(kv_chain, 1)
                act.wait_ge(kv_chain, i + 1)
                nc.scalar.activation(kss[0:m, 1, i:i + 1], kss[0:m, 0, i:i + 1], ACT.Sqrt, scale=1.0 / KV,
                                     bias=rms_eps[0:m]).then_inc(kv_sq, 1)
            for c in range(4):
                act.wait_ge(cq_done, c + 1)
                nc.scalar.activation(cqT[:, c], B[c % 2][:, 0:T], ACT.Copy)
                if c >= 2:
                    act.wait_ge(cq_sq_used, c - 1)
                nc.scalar.activation(sqq[c % 2], B[c % 2][:, 0:T], ACT.Square).then_inc(cq_copied, 1)
            act.wait_ge(cq_var, 1)
            nc.scalar.activation(rq, rq, ACT.Sqrt).then_inc(cq_std, 1)
            act.wait_ge(kv_ready, 3)
            for i, (t0, m) in enumerate(TILES):
                for name, src in (("ckv", ckv_tok[0:m, i]), ("kpe", kpe_tok[0:m, i, 0:ROPE])):
                    dst = a[name + "_prompt"][0, t0:t0 + m] if i < 2 else \
                        a[name + "_sample"].rearrange("b s r -> (b s) r")
                    act.dma_start(dst, src).then_inc(out_stored, 16)
            for h in range(NH):
                act.wait_ge(q_done, h + 1)
                nc.scalar.activation(qT[:, h], B[h % 2][:, 0:T], ACT.Copy).then_inc(qT_copied, 1)
            for g in range(4):
                act.wait_ge(uk_turned, g + 1)
                nc.scalar.activation(ukT[:, 2 * g:2 * g + 2], B[7 if g % 2 == 0 else 2].rearrange("p (h r) -> p h r", h=2),
                                     ACT.Copy).then_inc(uk_copied, 1)
            for h in range(NH + 1):
                if h < NH:
                    act.wait_ge(ql_done, h + 1)
                    if h >= 2:
                        act.wait_ge(s_done, h - 1)
                        act.wait_ge(staged, h - 1)
                    for c in range(2):
                        last = nc.scalar.activation(q_lat[h % 2][:, c], B[2 * (h % 2) + c][:, 0:T], ACT.Copy)
                    last.then_inc(ql_copied, 1)
                if h >= 1:
                    act.wait_ge(p_turned, h)
                    if h >= 2:
                        act.wait_ge(pv_done, h - 1)
                    nc.scalar.activation(pT[:], B[5][:, 0:384], ACT.Copy).then_inc(p_copied, 1)
                if h < NH:
                    act.wait_ge(s_max, h + 1)
                    for b, (lo, hi) in enumerate(((0, 128), (128, 384))):
                        last = nc.scalar.activation(sc[h % 2][:, lo:hi], sc[h % 2][:, lo:hi], ACT.Exp, scale=SCALE,
                                                    bias=sm[:, h % 2, 2 + b:3 + b], accum_out=sm[:, h % 2, 4 + b:5 + b])
                        last.then_inc(e_done, 1)
            act.wait_ge(ql_done, NH)
            act.dma_start(wuv, a["s_w_uv"].rearrange("(c p) h v -> p c (h v)", p=P)).then_inc(ld_uv, 16)
            act.wait_ge(p_turned, NH)
            act.dma_start(own, a["c_own"]).then_inc(own_ready, 16)

            def copy_keys(p):
                for n in range(0, 12, 2):
                    act.wait_ge(kt_turned, 12 * p + n + 1)
                    dst, rows = kt_place(n)
                    nc.scalar.activation(dst, B[0][0:rows, :], ACT.Copy).then_inc(kt_a, 1)

            copy_keys(0)
            for p in range(DB // 2):
                act.wait_ge(ss_max, p + 1)
                nc.scalar.activation(probs, wide[:, :], ACT.Exp, scale=SCALE, bias=sm[:, 0, 2:3],
                                     accum_out=sm[:, 0, 4:5]).then_inc(se_done, 1)
                nc.scalar.activation(probs_new, probs_new, ACT.Exp, scale=SCALE, bias=sm[:, 0, 2:3],
                                     accum_out=sm[:, 0, 5:6]).then_inc(se_done, 1)
                if p + 1 < DB // 2:
                    copy_keys(p + 1)
                for g in range(2):
                    act.wait_ge(sp_turned, 3 * p + g + 1)
                    nc.scalar.activation(pTs[:, 4 * g:4 * g + 4], B[5 + g].rearrange("p (j q) -> p j q", j=4), ACT.Copy)\
                        .then_inc(sp_a, 1)
            for h in range(NH):
                act.wait_ge(uv_done, h + 1)
                nc.scalar.activation(oT[:, h], B[5 if h % 2 == 0 else 7][:, 0:T], ACT.Copy).then_inc(oT_copied, 1)
            act_norm(act, 2)

        def kt_place(n):
            if n < 8:
                b, c, half = n // 4, n // 2 % 2, n % 2
                return KTs[b][c][:, half * 512:(half + 1) * 512], P
            b, half = (n - 8) // 2, n % 2
            return KPs[0:ROPE, b, half * 512:(half + 1) * 512], ROPE

        def pe_attention(pe):
            turn_x(pe, 2, 1)
            pe.wait_ge(ld_kv, 32)
            pe.wait_ge(xT_copied, 18)
            for i, (t0, m) in enumerate(TILES):
                for k in range(KD):
                    last = nc.tensor.matmul(B[2 + i][0:m, 0:KV + ROPE], xT[:, k, t0:t0 + m], wkv[:, k],
                                            start=(k == 0), stop=(k == KD - 1))
                last.then_inc(kv_done, 1)
            pe.wait_ge(ld_q, 16)

            def add_squares(c):
                pe.wait_ge(cq_copied, c + 1)
                if c == 0:
                    pe.wait_ge(kv_ready, 1)
                nc.tensor.matmul(B[2][:, 0:T], ones[:], sqq[c % 2], start=(c == 0), stop=(c == 3)).then_inc(cq_sq_used, 1)

            for c in range(4):
                if c >= 2:
                    pe.wait_ge(cq_copied, c - 1)
                for k in range(KD):
                    last = nc.tensor.matmul(B[c % 2][:, 0:T], wdq[:, k, c * P:(c + 1) * P], xT[:, k], start=(k == 0),
                                            stop=(k == KD - 1))
                last.then_inc(cq_done, 1)
                if c:
                    add_squares(c - 1)
            add_squares(3)
            pe.wait_ge(kv_ready, 3)
            for n in range(3):
                for i, (t0, m) in enumerate(TILES):
                    src = ckv_tok[0:m, i, n * P:(n + 1) * P] if n < 2 else kpe_tok[0:m, i]
                    last = nc.tensor.transpose(B[5 + n][:, t0:t0 + m], src, ident[0:m, 0:m])
                last.then_inc(c_turned, 1)
            pe.wait_ge(ld_uq, 16)
            for h in range(NH):
                pe.wait_ge(cq_copied, 4)
                if h >= 2:
                    pe.wait_ge(qT_copied, h - 1)
                for k in range(4):
                    pe.wait_ge(cq_ready, k + 1)
                    last = nc.tensor.matmul(B[h % 2][:, 0:T], wuq[:, k, h * 192:h * 192 + NOPE], cqT[:, k],
                                            start=(k == 0), stop=(k == 3))
                last.then_inc(q_done, 1)

            def swapped(p):
                pe.wait_ge(qpe_raw, p + 1)
                if p >= 2:
                    pe.wait_ge(qpe_ready, p - 1)
                nc.tensor.matmul(B[5 + p % 2][:, 0:T], swap, q_peT[:, p], start=True, stop=True).then_inc(qpe_swapped, 1)

            pe.wait_ge(ld_att, 64)
            pe.wait_ge(kT_copied, 3)
            for p in range(4):
                if p >= 2:
                    pe.wait_ge(qpe_raw, p - 1)
                for k in range(4):
                    for n in range(2):
                        h = 2 * p + n
                        last = nc.tensor.matmul(B[3 + p % 2][n * C:(n + 1) * C, 0:T],
                                                wuq[:, k, h * 192 + NOPE:(h + 1) * 192], cqT[:, k],
                                                start=(k == 0), stop=(k == 3))
                last.then_inc(qpe_done, 1)
                if p:
                    swapped(p - 1)
            swapped(3)
            pe.wait_ge(ld_uk, 16)
            for g in range(4):
                if g >= 2:
                    pe.wait_ge(uk_copied, g - 1)
                for n in range(4):
                    h, c = 2 * g + n // 2, n % 2
                    last = nc.tensor.transpose(B[7 if g % 2 == 0 else 2][:, n * P:(n + 1) * P],
                                               wuk[:, c, h * P:(h + 1) * P], ident[:])
                last.then_inc(uk_turned, 1)
            pe.wait_ge(uk_copied, 4)
            pe.wait_ge(qT_copied, NH)
            pe.wait_ge(qpe_ready, 4)
            for h in range(NH + 1):
                if h < NH:
                    if h >= 2:
                        pe.wait_ge(ql_copied, h - 1)
                    for c in range(2):
                        last = nc.tensor.matmul(B[2 * (h % 2) + c][:, 0:T], ukT[:, h, c * P:(c + 1) * P], qT[:, h],
                                                start=True, stop=True)
                    last.then_inc(ql_done, 1)
                if h >= 1:
                    pe.wait_ge(p_ready, h)
                    if h >= 2:
                        pe.wait_ge(p_copied, h - 1)
                    for n in range(3):
                        last = nc.tensor.transpose(B[5][:, n * P:(n + 1) * P], sc[(h - 1) % 2][:, n * P:(n + 1) * P],
                                                   ident[:])
                    last.then_inc(p_turned, 1)
                if h < NH:
                    pe.wait_ge(ql_copied, h + 1)
                    if h >= 2:
                        pe.wait_ge(s_read, h - 1)
                    bank = B[4 if h % 2 == 0 else 7]
                    r0 = (h % 2) * ROPE
                    for qb, (lo, hi) in enumerate(((0, 128), (128, 384))):
                        n = hi - lo
                        for c in range(2):
                            nc.tensor.matmul(bank[:, lo:hi], q_lat[h % 2][:, c, qb * P:(qb + 1) * P], kT[:, c, 0:n],
                                             start=(c == 0), stop=False)
                        last = nc.tensor.matmul(bank[:, lo:hi], q_peT[r0:r0 + ROPE, h // 2, qb * P:(qb + 1) * P],
                                                kpeT[r0:r0 + ROPE, 0:n], start=False, stop=True)
                    last.then_inc(s_done, 1)
                if h >= 1:
                    pe.wait_ge(p_copied, h)
                    if h >= 2:
                        pe.wait_ge(ol_copied, h - 1)
                    for c in range(2):
                        nc.tensor.matmul(B[6][:, c * 256:(c + 1) * 256], ckv_tok[:, 0, c * P:(c + 1) * P], pT[:, 0:256],
                                         start=True, stop=False)
                        last = nc.tensor.matmul(B[6][:, c * 256 + P:(c + 1) * 256], ckv_tok[:, 1, c * P:(c + 1) * P],
                                                pT[:, 256:384], start=False, stop=True)
                    last.then_inc(pv_done, 1)
            pe.wait_ge(ql_copied, NH)
            pe.wait_ge(s_read, NH)
            pe.wait_ge(ol_copied, NH)
            def turn_keys(p):
                pe.wait_ge(cache_ready[p % 2], (p // 2 + 1) * 32 * NPG)
                for n in range(12):
                    if n == 8:
                        pe.wait_ge(cpe_ready[p % 2], (p // 2 + 1) * 32 * NPG)
                    if p or n >= 2:
                        pe.wait_ge(kt_a if n % 2 == 0 else kt_d, 6 * p + n // 2)
                    for j in range(4):
                        if n < 8:
                            b, c, half = n // 4, n // 2 % 2, n % 2
                            src = cache[p % 2][:, b * NPG + half * 4 + j, c * P:(c + 1) * P]
                        else:
                            b, half = (n - 8) // 2, n % 2
                            src = cpe[p % 2][:, b * NPG + half * 4 + j]
                        last = nc.tensor.transpose(B[n % 2][0:(P if n < 8 else ROPE), j * P:(j + 1) * P], src, ident[:])
                    last.then_inc(kt_turned, 1)

            def score(p):
                pe.wait_ge(kt_a, 6 * (p + 1))
                pe.wait_ge(kt_d, 6 * (p + 1))
                if p == 0:
                    pe.wait_ge(staged, NH)
                for half in range(3):
                    if half == 2 and p:
                        pe.wait_ge(ols_ready, p)
                    for c in range(3):
                        for b in range(2):
                            rows = slice(0, P if c < 2 else ROPE)
                            if half < 2:
                                dst = wide[b * NS:(b + 1) * NS, half * 512:(half + 1) * 512]
                                key = KTs[b][c][:, half * 512:(half + 1) * 512] if c < 2 else \
                                    KPs[0:ROPE, b, half * 512:(half + 1) * 512]
                            else:
                                dst = B[4][b * NS:(b + 1) * NS, KV:KV + NS]
                                key = kT[:, c, SEQ:T] if c < 2 else kpeT[0:ROPE, SEQ:T]
                            last = nc.tensor.matmul(dst, q_stage[rows, c, p, b * NS:(b + 1) * NS], key, start=(c == 0),
                                                    stop=(c == 2))
                last.then_inc(ss_done, 1)

            def turn_out(p):
                pe.wait_ge(ols_ready, p + 1)
                for c in range(2):
                    last = nc.tensor.transpose(B[7][:, c * P:(c + 1) * P], ols[:, c * P:(c + 1) * P], ident[:])
                last.then_inc(ols_turned, 1)

            turn_keys(0)
            for p in range(DB // 2):
                score(p)
                if p:
                    turn_out(p - 1)
                if p + 1 < DB // 2:
                    turn_keys(p + 1)
                pe.wait_ge(se_done, 2 * p + 2)
                if p:
                    pe.wait_ge(ols_copied, 4 * p)
                for g in range(2):
                    for j in range(4):
                        last = nc.tensor.transpose(B[5 + g][:, j * P:(j + 1) * P],
                                                   probs[:, (4 * g + j) * P:(4 * g + j + 1) * P], ident[:])
                    last.then_inc(sp_turned, 1)
                nc.tensor.transpose(B[7][0:NS, 0:P], probs_new, ident[:]).then_inc(sp_turned, 1)
                pe.wait_ge(sp_a, 2 * p + 2)
                pe.wait_ge(sp_d, p + 1)
                for j in range(NPG):
                    for b in range(2):
                        nc.tensor.matmul(B[4][b * NS:(b + 1) * NS, 0:KV], pTs[:, j, b * NS:(b + 1) * NS],
                                         cache[p % 2][:, b * NPG + j], start=(j == 0), stop=False)
                for b in range(2):
                    last = nc.tensor.matmul(B[4][b * NS:(b + 1) * NS, 0:KV], pTn[0:NS, b * NS:(b + 1) * NS],
                                            ckv_tok[0:NS, 2], start=False, stop=True)
                last.then_inc(pair_done, 1)
            turn_out(DB // 2 - 1)
            pe.wait_ge(ld_uv, 16)
            pe.wait_ge(ols_copied, 4 * (DB // 2))
            for h in range(NH):
                if h >= 2:
                    pe.wait_ge(oT_copied, h - 1)
                for c in range(2):
                    last = nc.tensor.matmul(B[5 if h % 2 == 0 else 7][:, 0:T], wuv[:, c, h * P:(h + 1) * P],
                                            olT[:, c, h], start=(c == 0), stop=(c == 1))
                last.then_inc(uv_done, 1)
            pe.wait_ge(ld_o, 16)
            out_product(pe, oT, wo, oT_copied, 8)

        def dve_attention(dve, after, mark, seq):
            V = nc.vector
            dve.wait_ge(ld_att, 64)
            for i, (t0, m) in enumerate(TILES):
                dve.wait_ge(kv_sq, i + 1)
                after(V.reciprocal(kss[0:m, 1, i:i + 1], kss[0:m, 1, i:i + 1]))
                after(V.scalar_tensor_tensor(ckv_tok[0:m, i], B[2 + i][0:m, 0:KV], kss[0:m, 1, i:i + 1], gkv[0:m],
                                             ALU.mult, ALU.mult))
                x1, x2 = B[2 + i][0:m, KV:KV + HALF], B[2 + i][0:m, KV + HALF:KV + ROPE]
                cos, sin = rope_tok[0:m, i, 0], rope_tok[0:m, i, 1]
                o1, o2 = kpe_tok[0:m, i, 0:HALF], kpe_tok[0:m, i, HALF:ROPE]
                mark(V.tensor_tensor(o1, x1, cos, ALU.mult))
                mark(V.tensor_tensor(k_tmp[0:m, 0], x2, sin, ALU.mult))
                mark(V.tensor_tensor(o2, x2, cos, ALU.mult))
                after(V.tensor_tensor(k_tmp[0:m, 1], x1, sin, ALU.mult))
                mark(V.tensor_tensor(o1, o1, k_tmp[0:m, 0], ALU.subtract))
                after(V.tensor_tensor(o2, o2, k_tmp[0:m, 1], ALU.add))
                V.tensor_copy(kpe_tok[0:m, i, ROPE:], kpe_tok[0:m, i, 0:ROPE]).then_inc(kv_ready, 1)
            dve.wait_ge(cq_sq_used, 4)
            V.tensor_scalar(rq, B[2][:, 0:T], 1.0 / QR, RMS_EPS, ALU.mult, ALU.add).then_inc(cq_var, 1)
            dve.wait_ge(cq_std, 1)
            after(V.reciprocal(rq, rq))
            for c in range(4):
                V.scalar_tensor_tensor(cqT[:, c], cqT[:, c], vec_T[:, 40 + c:41 + c], rq, ALU.mult, ALU.mult)\
                    .then_inc(cq_ready, 1)
            for n, dst in enumerate((kT[:, 0], kT[:, 1], kpeT)):
                dve.wait_ge(c_turned, n + 1)
                V.tensor_copy(dst, B[5 + n][:, 0:T]).then_inc(kT_copied, 1)

            def rotate(p):
                dve.wait_ge(qpe_swapped, p + 1)
                mark(V.tensor_tensor(q_tmp, B[5 + p % 2][:, 0:T], rope_T[:, 1], ALU.mult))
                after(V.tensor_tensor(q_peT[:, p], q_peT[:, p], rope_T[:, 0], ALU.mult))
                ins = V.tensor_tensor(q_peT[:, p], q_peT[:, p], q_tmp, ALU.add)
                ins.then_inc(qpe_ready, 1)

            for p in range(4):
                dve.wait_ge(qpe_done, p + 1)
                V.tensor_copy(q_peT[:, p], B[3 + p % 2][:, 0:T]).then_inc(qpe_raw, 1)
                if p:
                    if p >= 2:
                        dve.wait_ge(qpe_ready, p - 1)
                    rotate(p - 1)
            dve.wait_ge(qpe_ready, 3)
            rotate(3)
            for h in range(NH + 1):
                s = h % 2
                if h < NH:
                    dve.wait_ge(s_done, h + 1)
                    if h >= 2:
                        dve.wait_ge(p_turned, h - 1)
                    V.tensor_tensor(sc[s], B[4 if s == 0 else 7][:, 0:384], causal[:], ALU.add).then_inc(s_read, 1)
                    dve.wait_ge(s_read, h + 1)
                    mark(V.tensor_reduce(sm[:, s, 0:1], sc[s][:, 0:128], AX.X, ALU.max))
                    after(V.tensor_reduce(sm[:, s, 1:2], sc[s][:, 128:384], AX.X, ALU.max))
                    V.tensor_scalar(sm[:, s, 2:4], sm[:, s, 0:2], -SCALE, None, ALU.mult).then_inc(s_max, 1)
                    dve.wait_ge(ql_copied, h + 1)
                    for c in range(3):
                        if c < 2:
                            src, dst = q_lat[s][:, c, SEQ:T], q_stage[:, c]
                        else:
                            dve.wait_ge(qpe_ready, 4)
                            src, dst = q_peT[s * ROPE:(s + 1) * ROPE, h // 2, SEQ:T], q_stage[0:ROPE, c]
                        dst = dst.rearrange("p n (b h t) -> p (n b) h t", b=2, h=NH)[:, :, h]
                        last = V.tensor_copy(dst, src.rearrange("p (b t) -> p b t", t=DS))
                    last.then_inc(staged, 1)
                if h >= 1:
                    dve.wait_ge(pv_done, h)
                    V.tensor_copy(olT[:, :, h - 1, 0:SEQ], B[6].rearrange("p (c q) -> p c q", c=2)).then_inc(ol_copied, 1)
                if h < NH:
                    dve.wait_ge(e_done, 2 * h + 2)
                    after(V.reciprocal(sm[:, s, 6:8], sm[:, s, 4:6]))
                    mark(V.tensor_scalar(sc[s][:, 0:128], sc[s][:, 0:128], sm[:, s, 6:7], None, ALU.mult))
                    V.tensor_scalar(sc[s][:, 128:384], sc[s][:, 128:384], sm[:, s, 7:8], None, ALU.mult)\
                        .then_inc(p_ready, 1)
            dve.wait_ge(staged, NH)

            def copy_keys(p):
                for n in range(1, 12, 2):
                    dve.wait_ge(kt_turned, 12 * p + n + 1)
                    dst, rows = kt_place(n)
                    V.tensor_copy(dst, B[1][0:rows, :]).then_inc(kt_d, 1)

            def copy_out(p):
                dve.wait_ge(ols_turned, p + 1)
                for c in range(2):
                    for b in range(2):
                        dst = olT[:, c].rearrange("p h (n t) -> p h n t", t=DS)[:, :, SEQ // DS + 2 * p + b]
                        V.tensor_copy(dst, B[7][:, c * P + b * NS:c * P + (b + 1) * NS]
                                      .rearrange("p (h t) -> p h t", h=NH)).then_inc(ols_copied, 1)

            copy_keys(0)
            dve.wait_ge(own_ready, 16)
            for p in range(DB // 2):
                dve.wait_ge(ss_done, p + 1)
                mark(V.tensor_tensor(probs_new, B[4][:, KV:KV + NS], own[:, p], ALU.add))
                after(V.tensor_reduce(sm[:, 0, 0:1], wide[:, :], AX.X, ALU.max))
                after(V.tensor_reduce(sm[:, 0, 1:2], probs_new, AX.X, ALU.max))
                after(V.tensor_reduce(sm[:, 1, 0:1], sm[:, 0, 0:2], AX.X, ALU.max))
                V.tensor_scalar(sm[:, 0, 2:3], sm[:, 1, 0:1], -SCALE, None, ALU.mult).then_inc(ss_max, 1)
                if p:
                    copy_out(p - 1)
                if p + 1 < DB // 2:
                    copy_keys(p + 1)
                dve.wait_ge(se_done, 2 * p + 2)
                after(V.tensor_tensor(sm[:, 0, 6:7], sm[:, 0, 4:5], sm[:, 0, 5:6], ALU.add))
                mark(V.reciprocal(sm[:, 0, 7:8], sm[:, 0, 6:7]))
                dve.wait_ge(sp_turned, 3 * p + 3)
                V.tensor_copy(pTn[0:NS], B[7][0:NS, 0:P]).then_inc(sp_d, 1)
                dve.wait_ge(dve_seq, seq[0])
                dve.wait_ge(pair_done, p + 1)
                V.tensor_scalar(ols, B[4][:, 0:KV], sm[:, 0, 7:8], None, ALU.mult).then_inc(ols_ready, 1)
            copy_out(DB // 2 - 1)

        block = ctx.enter_context(nc.Block())
        block.sync(sp_program)
        block.gpsimd(pool_program)
        block.scalar(act_program)
        block.tensor(pe_program)
        block.vector(dve_program)


_INS = ['x_prompt', 'x_sample', 'state_conv', 'cache_ckv', 'cache_kpe', 'page_table', 'a_w_pw1', 'a_b_pw1', 'a_w_dw',
        'a_b_dw', 'a_g_cn', 'a_b_cn', 'a_w_pw2', 'a_b_pw2', 'ln_mix_g', 'ln_mix_b', 'ln_ffn_g', 'ln_ffn_b', 'b_w_dq',
        'b_g_q', 'b_w_uq', 'b_w_o', 's_w_dkv', 's_g_kv', 's_w_kr', 's_w_uk', 's_w_uv', 'r_w', 'r_b', 'e_w1', 'e_w3',
        'e_w2']
_OUTS = {
    "y_prompt": (1, SEQ, D), "y_sample": (DB, DS, D), "conv_prompt": (1, 1, CS, D), "conv_sample": (1, DB, CS, D),
    "ckv_prompt": (1, SEQ, KV), "kpe_prompt": (1, SEQ, ROPE), "ckv_sample": (DB, DS, KV), "kpe_sample": (DB, DS, ROPE),
}


def kernel(**inputs):
    import concourse.bacc as bacc
    from concourse.bass_utils import run_bass_kernel_spmd

    nc = bacc.Bacc("TRN2", target_bir_lowering=False, num_devices=1)
    arrays, aps = {}, {}
    given = {name: np.ascontiguousarray(inputs[name]) for name in _INS}
    given.update(tables())
    for name, v in given.items():
        arrays[f"in_{name}"] = v
        aps[name] = nc.dram_tensor(f"in_{name}", v.shape, mybir.dt.from_np(v.dtype), kind="ExternalInput").ap()
    for name, shape in _OUTS.items():
        aps[name] = nc.dram_tensor(f"out_{name}", shape, F32, kind="ExternalOutput").ap()
    trunk_step(nc, aps)
    r = run_bass_kernel_spmd(nc, [arrays], core_ids=[0])
    return tuple(r.results[0][f"out_{name}"] for name in _OUTS)
```
